# Optimizing a Trainium2 kernel written in Bass

```python
import jax
import jax.numpy as jnp
from jax import lax
import numpy as np

D_MODEL = 1024
BATCH = 1
SEQ = 512
DEPTH = 2
DEC_BATCH = 8
DEC_SEQ = 4
PAST_LEN = 4096
PAGE_SIZE = 128

POOL_WIDTH = 256
POOL_WINDOWS = (2, 4, 8, 16)
POOL_GROUPS = 4
POOL_GROUP_DIM = POOL_WIDTH // POOL_GROUPS
POOL_HIST = max(POOL_WINDOWS) - 1
CONV_WIDTH = 256
CONV_K = 31
CONV_HIST = CONV_K - 1
N_HEADS = 8
QK_NOPE = 64
QK_ROPE = 32
V_HEAD = 64
Q_LORA = 192
KV_LORA = 128
ROPE_BASE = 10000.0
Q_BLOCK = 128
SCONV_WIDTH = 256
SCONV_K = 3
SCONV_HIST = SCONV_K - 1
N_BRANCH = 4
IN_COLS = POOL_WIDTH + 2 * CONV_WIDTH + Q_LORA + KV_LORA + QK_ROPE + 3 * SCONV_WIDTH + N_BRANCH * D_MODEL
N_GROUPS = 4
EXPERTS_PER_GROUP = 4
N_EXPERTS = N_GROUPS * EXPERTS_PER_GROUP
TOP_K = 2
D_FF_EXPERT = 256
ALPHA = (2 * DEPTH) ** 0.25
BETA = (8 * DEPTH) ** -0.25
LN_EPS = 1e-5
RMS_EPS = 1e-6

kernel_name = 'hybrid_pool_conv_mla_shortconv_hmoe_step'

def layer_norm(x, g, b):
    xf = x.astype(jnp.float32)
    mu = jnp.mean(xf, axis=-1, keepdims=True)
    var = jnp.mean(jnp.square(xf - mu), axis=-1, keepdims=True)
    return ((xf - mu) * lax.rsqrt(var + LN_EPS) * g.astype(jnp.float32) + b.astype(jnp.float32)).astype(x.dtype)

def rms_norm(x, g):
    xf = x.astype(jnp.float32)
    return (xf * lax.rsqrt(jnp.mean(jnp.square(xf), axis=-1, keepdims=True) + RMS_EPS) * g.astype(jnp.float32)).astype(x.dtype)

def rope(x, pos):
    half = x.shape[-1] // 2
    inv_freq = ROPE_BASE ** (-jnp.arange(half, dtype=jnp.float32) / half)
    ang = pos.astype(jnp.float32)[:, None] * inv_freq[None, :]
    shp = (1, pos.shape[0]) + (1,) * (x.ndim - 3) + (half,)
    cos, sin = jnp.cos(ang).reshape(shp), jnp.sin(ang).reshape(shp)
    xf = x.astype(jnp.float32)
    x1, x2 = xf[..., :half], xf[..., half:]
    return jnp.concatenate([x1 * cos - x2 * sin, x1 * sin + x2 * cos], axis=-1).astype(x.dtype)

def depthwise_causal_conv(xp, w):
    return lax.conv_general_dilated(xp, w[:, None, :], window_strides=(1,), padding='VALID',
                                    dimension_numbers=('NWC', 'WIO', 'NWC'),
                                    feature_group_count=xp.shape[-1])

def pool_mixer(u, hist, pos, w, scale):
    bsz, t_len, _ = u.shape
    xp = jnp.concatenate([hist, u], axis=1)
    cs = jnp.cumsum(xp.astype(jnp.float32), axis=1)
    cs = jnp.concatenate([jnp.zeros_like(cs[:, :1]), cs], axis=1)
    end = cs[:, POOL_HIST + 1:]
    means = []
    for g, win in enumerate(POOL_WINDOWS):
        sl = slice(g * POOL_GROUP_DIM, (g + 1) * POOL_GROUP_DIM)
        start = cs[:, POOL_HIST + 1 - win:POOL_HIST + 1 - win + t_len, sl]
        cnt = jnp.minimum(win, pos + 1).astype(jnp.float32)[None, :, None]
        means.append((end[..., sl] - start) / cnt)
    pooled = (jnp.concatenate(means, axis=-1) - u.astype(jnp.float32)).astype(u.dtype)
    mixed = jnp.einsum('btgc,gcd->btgd', pooled.reshape(bsz, t_len, POOL_GROUPS, POOL_GROUP_DIM), w)
    return mixed.reshape(bsz, t_len, POOL_WIDTH) * scale, xp[:, -POOL_HIST:]

def conformer_conv(u, hist, w, b, ln_g, ln_b):
    glu = u[..., :CONV_WIDTH] * jax.nn.sigmoid(u[..., CONV_WIDTH:])
    xp = jnp.concatenate([hist, glu], axis=1)
    y = depthwise_causal_conv(xp, w) + b
    return jax.nn.silu(layer_norm(y, ln_g, ln_b)), xp[:, -CONV_HIST:]

def short_conv(u, hist, w):
    bg, cg, h = jnp.split(u, 3, axis=-1)
    xp = jnp.concatenate([hist, cg * h], axis=1)
    return bg * depthwise_causal_conv(xp, w), xp[:, -SCONV_HIST:]

def mla_attend(q_lat, q_rope, ckv, krope, q_pos, k_pos):
    scale = (QK_NOPE + QK_ROPE) ** -0.5

    def attend_block(ql, qr, qp):
        s = jnp.einsum('bthc,blc->bhtl', ql, ckv) + jnp.einsum('bthr,blr->bhtl', qr, krope)
        s = s.astype(jnp.float32) * scale
        s = jnp.where(qp[:, None] >= k_pos[None, :], s, -1e30)
        p = jax.nn.softmax(s, axis=-1).astype(ckv.dtype)
        return jnp.einsum('bhtl,blc->bthc', p, ckv)

    bsz, t_len, n_h, c_dim = q_lat.shape
    if t_len > Q_BLOCK and t_len % Q_BLOCK == 0:
        nb = t_len // Q_BLOCK
        blk = lambda a: jnp.moveaxis(a.reshape((bsz, nb, Q_BLOCK) + a.shape[2:]), 1, 0)
        out = lax.map(lambda args: attend_block(*args),
                      (blk(q_lat), blk(q_rope), q_pos.reshape(nb, Q_BLOCK)))
        return jnp.moveaxis(out, 0, 1).reshape(bsz, t_len, n_h, c_dim)
    return attend_block(q_lat, q_rope, q_pos)

def token_mixer(x, pos, past_ckv, past_krope, h_pool, h_conv, h_sconv,
                w_in, pool_w, pool_scale, conv_w, conv_b, conv_ln_g, conv_ln_b,
                q_norm_g, kv_norm_g, w_uq, w_uk, w_uv, sconv_w,
                p_pool, p_conv, p_attn, p_sconv, w_o):
    bsz, t_len, _ = x.shape
    proj = x @ w_in
    bounds = [int(v) for v in np.cumsum([POOL_WIDTH, 2 * CONV_WIDTH, Q_LORA, KV_LORA, QK_ROPE, 3 * SCONV_WIDTH])]
    u_pool, u_glu, u_qa, u_kva, u_kr, u_sc, u_gate = jnp.split(proj, bounds, axis=-1)
    a_out, pool_state = pool_mixer(u_pool, h_pool, pos, pool_w, pool_scale)
    b_out, conv_state = conformer_conv(u_glu, h_conv, conv_w, conv_b, conv_ln_g, conv_ln_b)
    q = (rms_norm(u_qa, q_norm_g) @ w_uq).reshape(bsz, t_len, N_HEADS, QK_NOPE + QK_ROPE)
    q_nope, q_rope = q[..., :QK_NOPE], rope(q[..., QK_NOPE:], pos)
    ckv = rms_norm(u_kva, kv_norm_g)
    krope = rope(u_kr, pos)
    q_lat = jnp.einsum('bthn,chn->bthc', q_nope, w_uk)
    keys_ckv = jnp.concatenate([past_ckv, ckv], axis=1)
    keys_kr = jnp.concatenate([past_krope, krope], axis=1)
    k_pos = jnp.arange(keys_ckv.shape[1], dtype=jnp.int32)
    lat = mla_attend(q_lat, q_rope, keys_ckv, keys_kr, pos, k_pos)
    c_out = jnp.einsum('bthc,chv->bthv', lat, w_uv).reshape(bsz, t_len, N_HEADS * V_HEAD)
    d_out, sconv_state = short_conv(u_sc, h_sconv, sconv_w)
    g = jax.nn.sigmoid(u_gate).reshape(bsz, t_len, N_BRANCH, D_MODEL)
    merged = (g[:, :, 0] * (a_out @ p_pool) + g[:, :, 1] * (b_out @ p_conv)
              + g[:, :, 2] * (c_out @ p_attn) + g[:, :, 3] * (d_out @ p_sconv))
    return merged @ w_o, (ckv, krope, pool_state, conv_state, sconv_state)

def hier_moe(x, router_g, router_g_b, router_e, router_e_b, w_gate, w_up, w_down):
    bsz, t_len, _ = x.shape
    gl = (x @ router_g).astype(jnp.float32) + router_g_b.astype(jnp.float32)
    pg = jax.nn.softmax(gl, axis=-1)
    g_idx = jnp.argmax(gl, axis=-1)
    g_w = jnp.take_along_axis(pg, g_idx[..., None], axis=-1)
    el = ((x @ router_e).astype(jnp.float32) + router_e_b.astype(jnp.float32)).reshape(bsz, t_len, N_GROUPS, EXPERTS_PER_GROUP)
    el_sel = jnp.take_along_axis(el, g_idx[..., None, None], axis=2)[:, :, 0]
    top_w, top_i = lax.top_k(jax.nn.softmax(el_sel, axis=-1), TOP_K)
    top_w = top_w / jnp.sum(top_w, axis=-1, keepdims=True) * g_w
    expert_id = g_idx[..., None] * EXPERTS_PER_GROUP + top_i
    comb = jnp.sum(jax.nn.one_hot(expert_id, N_EXPERTS, dtype=jnp.float32) * top_w[..., None], axis=-2)
    h = jax.nn.silu(jnp.einsum('btd,edf->btef', x, w_gate)) * jnp.einsum('btd,edf->btef', x, w_up)
    h = h * comb.astype(x.dtype)[..., None]
    return jnp.einsum('btef,efd->btd', h, w_down)

def decoder_layer(x, pos, past_ckv, past_krope, h_pool, h_conv, h_sconv, mix_params, moe_params, ln_params):
    ln1_g, ln1_b, ln2_g, ln2_b = ln_params
    mix, st = token_mixer(x, pos, past_ckv, past_krope, h_pool, h_conv, h_sconv, *mix_params)
    x = layer_norm(ALPHA * x + mix, ln1_g, ln1_b)
    x = layer_norm(ALPHA * x + hier_moe(x, *moe_params), ln2_g, ln2_b)
    return x, st

def setup_inputs(seed: int = 0) -> dict:
    key = jax.random.key(seed)
    k = jax.random.split(key, 40)
    f32 = jnp.float32

    def nrm(i, shape, scale):
        return jax.random.normal(k[i], shape, f32) * scale

    def gain(i, shape):
        return 1.0 + nrm(i, shape, 0.05)

    n_pages = PAST_LEN // PAGE_SIZE
    n_pool = (5 * DEC_BATCH * n_pages) // 4
    page_table = jax.random.permutation(k[7], n_pool)[:DEC_BATCH * n_pages].reshape(DEC_BATCH, n_pages).astype(jnp.int32)
    L = DEPTH
    return {
        'x_prompt': nrm(0, (BATCH, SEQ, D_MODEL), 1.0),
        'x_sample': nrm(1, (DEC_BATCH, DEC_SEQ, D_MODEL), 1.0),
        'cache_ckv': nrm(2, (L, n_pool, PAGE_SIZE, KV_LORA), 1.0),
        'cache_krope': nrm(3, (L, n_pool, PAGE_SIZE, QK_ROPE), 1.0),
        'state_pool': nrm(4, (L, DEC_BATCH, POOL_HIST, POOL_WIDTH), 1.0),
        'state_conv': nrm(5, (L, DEC_BATCH, CONV_HIST, CONV_WIDTH), 1.0),
        'state_sconv': nrm(6, (L, DEC_BATCH, SCONV_HIST, SCONV_WIDTH), 1.0),
        'page_table': page_table,
        'ln1_g': gain(8, (L, D_MODEL)),
        'ln1_b': nrm(9, (L, D_MODEL), 0.02),
        'ln2_g': gain(10, (L, D_MODEL)),
        'ln2_b': nrm(11, (L, D_MODEL), 0.02),
        'w_in': nrm(12, (L, D_MODEL, IN_COLS), D_MODEL ** -0.5),
        'pool_w': nrm(13, (L, POOL_GROUPS, POOL_GROUP_DIM, POOL_GROUP_DIM), POOL_GROUP_DIM ** -0.5),
        'pool_scale': gain(14, (L, POOL_WIDTH)),
        'conv_w': nrm(15, (L, CONV_K, CONV_WIDTH), CONV_K ** -0.5),
        'conv_b': nrm(16, (L, CONV_WIDTH), 0.02),
        'conv_ln_g': gain(17, (L, CONV_WIDTH)),
        'conv_ln_b': nrm(18, (L, CONV_WIDTH), 0.02),
        'q_norm_g': gain(19, (L, Q_LORA)),
        'kv_norm_g': gain(20, (L, KV_LORA)),
        'w_uq': nrm(21, (L, Q_LORA, N_HEADS * (QK_NOPE + QK_ROPE)), Q_LORA ** -0.5),
        'w_uk': nrm(22, (L, KV_LORA, N_HEADS, QK_NOPE), KV_LORA ** -0.5),
        'w_uv': nrm(23, (L, KV_LORA, N_HEADS, V_HEAD), BETA * KV_LORA ** -0.5),
        'sconv_w': nrm(24, (L, SCONV_K, SCONV_WIDTH), SCONV_K ** -0.5),
        'p_pool': nrm(25, (L, POOL_WIDTH, D_MODEL), BETA * POOL_WIDTH ** -0.5),
        'p_conv': nrm(26, (L, CONV_WIDTH, D_MODEL), BETA * CONV_WIDTH ** -0.5),
        'p_attn': nrm(27, (L, N_HEADS * V_HEAD, D_MODEL), BETA * (N_HEADS * V_HEAD) ** -0.5),
        'p_sconv': nrm(28, (L, SCONV_WIDTH, D_MODEL), BETA * SCONV_WIDTH ** -0.5),
        'w_o': nrm(29, (L, D_MODEL, D_MODEL), BETA * D_MODEL ** -0.5),
        'router_g': nrm(30, (L, D_MODEL, N_GROUPS), D_MODEL ** -0.5),
        'router_g_b': nrm(31, (L, N_GROUPS), 0.01),
        'router_e': nrm(32, (L, D_MODEL, N_EXPERTS), D_MODEL ** -0.5),
        'router_e_b': nrm(33, (L, N_EXPERTS), 0.01),
        'exp_w_gate': nrm(34, (L, N_EXPERTS, D_MODEL, D_FF_EXPERT), D_MODEL ** -0.5),
        'exp_w_up': nrm(35, (L, N_EXPERTS, D_MODEL, D_FF_EXPERT), BETA * D_MODEL ** -0.5),
        'exp_w_down': nrm(36, (L, N_EXPERTS, D_FF_EXPERT, D_MODEL), BETA * D_FF_EXPERT ** -0.5),
    }

def reference(x_prompt, x_sample, cache_ckv, cache_krope, state_pool, state_conv, state_sconv, page_table,
              ln1_g, ln1_b, ln2_g, ln2_b, w_in, pool_w, pool_scale, conv_w, conv_b, conv_ln_g, conv_ln_b,
              q_norm_g, kv_norm_g, w_uq, w_uk, w_uv, sconv_w, p_pool, p_conv, p_attn, p_sconv, w_o,
              router_g, router_g_b, router_e, router_e_b, exp_w_gate, exp_w_up, exp_w_down):
    bp, tp, _ = x_prompt.shape
    bs, ts, _ = x_sample.shape
    past_len = page_table.shape[1] * cache_ckv.shape[2]
    pos_p = jnp.arange(tp, dtype=jnp.int32)
    pos_s = past_len + jnp.arange(ts, dtype=jnp.int32)
    dt_p = x_prompt.dtype
    zp_ckv = jnp.zeros((bp, 0, KV_LORA), dt_p)
    zp_kr = jnp.zeros((bp, 0, QK_ROPE), dt_p)
    zp_pool = jnp.zeros((bp, POOL_HIST, POOL_WIDTH), dt_p)
    zp_conv = jnp.zeros((bp, CONV_HIST, CONV_WIDTH), dt_p)
    zp_sconv = jnp.zeros((bp, SCONV_HIST, SCONV_WIDTH), dt_p)
    xp, xs = x_prompt, x_sample
    states_p, states_s = [], []
    for l in range(DEPTH):
        mix_params = (w_in[l], pool_w[l], pool_scale[l], conv_w[l], conv_b[l], conv_ln_g[l], conv_ln_b[l],
                      q_norm_g[l], kv_norm_g[l], w_uq[l], w_uk[l], w_uv[l], sconv_w[l],
                      p_pool[l], p_conv[l], p_attn[l], p_sconv[l], w_o[l])
        moe_params = (router_g[l], router_g_b[l], router_e[l], router_e_b[l],
                      exp_w_gate[l], exp_w_up[l], exp_w_down[l])
        ln_params = (ln1_g[l], ln1_b[l], ln2_g[l], ln2_b[l])
        xp, st_p = decoder_layer(xp, pos_p, zp_ckv, zp_kr, zp_pool, zp_conv, zp_sconv,
                                 mix_params, moe_params, ln_params)
        states_p.append(st_p)
        past_ckv = cache_ckv[l, page_table].reshape(bs, past_len, KV_LORA)
        past_kr = cache_krope[l, page_table].reshape(bs, past_len, QK_ROPE)
        xs, st_s = decoder_layer(xs, pos_s, past_ckv, past_kr, state_pool[l], state_conv[l], state_sconv[l],
                                 mix_params, moe_params, ln_params)
        states_s.append(st_s)
    sp = [jnp.stack(a, axis=0) for a in zip(*states_p)]
    ss = [jnp.stack(a, axis=0) for a in zip(*states_s)]
    return (xp, xs, sp[0], sp[1], sp[2], sp[3], sp[4], ss[0], ss[1], ss[2], ss[3], ss[4])


_drawn_inputs = setup_inputs


def setup_inputs(seed=0):
    import zlib

    import numpy as np

    out = dict(_drawn_inputs(seed))
    spreads = {}
    factors = {'cache_ckv': 8.0,
     'cache_krope': 8.0,
     'pool_scale': 7.953,
     'conv_b': 8.0,
     'conv_ln_g': 8.0,
     'conv_ln_b': 8.0,
     'q_norm_g': 8.0,
     'w_uq': 5.584,
     'w_uk': 6.029,
     'w_uv': 4.348,
     'p_attn': 4.374,
     'router_g_b': 8.0,
     'router_e_b': 8.0}
    for name, (base, spread) in spreads.items():
        noise = np.random.default_rng([zlib.crc32(name.encode()), seed]).standard_normal(out[name].shape)
        drawn = base * np.exp(spread * noise) if base else spread * noise
        out[name] = jnp.asarray(drawn.astype(out[name].dtype))
    for name, factor in factors.items():
        out[name] = (out[name] * factor).astype(out[name].dtype)
    return out
```

```python
from contextlib import ExitStack

import concourse.bass as bass
from concourse import mybir

ALU = mybir.AluOpType
ACT = mybir.ActivationFunctionType
AX = mybir.AxisListType
F32 = mybir.dt.float32
I32 = mybir.dt.int32

P = 128
D = 1024
KD = D // P
SEQ = 512
DB = 8
DS = 4
HP = SEQ // 2
HS = DB * DS // 2
HN = HP + HS
N = 2 * HN
DEPTH = 2
PAGE = 128
NPAGE = 32
POOLW, POOLH = 256, 15
CONVW, CONVK, CONVH = 256, 31, 30
NH, NOPE, ROPE, VH = 8, 64, 32, 64
QL, KVL = 192, 128
SCW, SCK, SCH = 256, 3, 2
NB = 4
NG, EPG, NE, FF = 4, 4, 16, 256
ALPHA = (2 * DEPTH) ** 0.25
LN_EPS, RMS_EPS = 1e-5, 1e-6
SCALE = (NOPE + ROPE) ** -0.5
NEG = -1e30

C_POOL, C_A, C_B = 0, 256, 512
C_QA = C_POOL + POOLW + 2 * CONVW
C_KV = C_QA + QL
C_SC = C_KV + KVL + ROPE
C_GATE = C_SC + 3 * SCW

SLOTS = 7
SLOT = 2048
GROUPS = NPAGE // 4
LOADS = GROUPS // 2
CACHES = 3


def columns(t, half, block):
    return t[:, half, block * P:(block + 1) * P]


def sample(t):
    return t[:, :, HP:HN].rearrange("p h (b t) -> p h b t", t=DS)


def prompt(t):
    return t[:, :, 0:HP]


class Chain:

    def __init__(self, engine, sem):
        self.engine, self.sem, self.n = engine, sem, 0

    def step(self, ins):
        ins.then_inc(self.sem, 1)
        self.n += 1

    def settle(self, behind=0):
        if self.n > behind:
            self.engine.wait_ge(self.sem, self.n - behind)


def slot_ready(k, pe, pos):
    pe.wait_ge(k.w_in[pos % SLOTS], 16 * (pos // SLOTS + 1))


def slot(k, pos, tiles, width):
    return k.ring[:, pos % SLOTS, 0:tiles * width].rearrange("p (k n) -> p k n", k=tiles)


def fill(k, sp, pos, tiles, width, src):
    if pos >= SLOTS:
        sp.wait_ge(k.w_free, pos - SLOTS + 1)
    sp.dma_start(slot(k, pos, tiles, width), src).then_inc(k.w_in[pos % SLOTS], 16)


POS_PROJ = 0
POS_BRANCH = 8
POS_WO = POS_BRANCH + 2 * NB * 4
POS_EXPERT = POS_WO + 4
POS_DOWN = POS_EXPERT + 2 * NE
POS_END = POS_DOWN + 16


def rows(t, l, tiles):
    return t[bass.ds(l, 1)].rearrange("a (k p) n -> p (a k) n", k=tiles)


def load_start(k):
    nc = k.nc

    @nc_block(nc)
    def _(block):
        @block.sync
        def _(sp):
            for i in range(4):
                sp.dma_start(k.xin[:, i, :], k.d["x_prompt"][0, i * P:(i + 1) * P, :]).then_inc(k.s_x[i], 16)
            for h in range(2):
                sp.dma_start(k.xins[0:HS, h, :],
                             k.d["x_sample"][4 * h:4 * h + 4].rearrange("b t d -> (b t) d")).then_inc(k.s_x[4], 16)

        @block.scalar
        def _(act):
            for dst, src in ((k.ident, k.d["c_ident"]), (k.rot, k.d["c_rot"]), (k.rotrep, k.d["c_rotrep"]),
                             (k.sel, k.d["c_sel"]), (k.cos, k.d["c_cos"]), (k.sin, k.d["c_sin"]),
                             (k.pcnt, k.d["c_pcnt"]), (k.cmask, k.d["c_cmask"]), (k.nmask, k.d["c_nmask"]),
                             (k.row, k.d["c_row"])):
                act.dma_start(dst[:], src).then_inc(k.s_const, 16)
            pt = k.d["page_table"].rearrange("b n -> (b n)")[None, :]
            act.dma_start(k.pages[:], pt.broadcast_to([P, DB * NPAGE])).then_inc(k.s_const, 16)
            act.wait_ge(k.s_const, 16 * 11)

        @block.gpsimd
        def _(pool):
            for i, (t, v) in enumerate(((k.ones, 1.0), (k.eps[:, 0:1], LN_EPS), (k.eps[:, 1:2], RMS_EPS),
                                        (k.wuv, 0.0), (k.poolw, 0.0))):
                pool.memset(t if i in (1, 2) else t[:], v).then_inc(k.s_set, 1)
            pool.wait_ge(k.s_set, 5)

        @block.tensor
        def _(pe):
            pe.wait_ge(k.s_const, 16 * 11)
            for u in range(8):
                pe.wait_ge(k.s_x[u // 2], 16)
                for j in range(4):
                    f = 4 * (u % 2) + j
                    t = nc.tensor.transpose(k.ps[:, u, j * P:(j + 1) * P], k.xin[:, u // 2, f * P:(f + 1) * P], k.ident[:])
                t.then_inc(k.s_xt, 1)
            pe.wait_ge(k.s_x[4], 32)
            for h in range(2):
                pe.wait_ge(k.s_xc, h + 1)
                for f in range(KD):
                    t = nc.tensor.transpose(k.ps[:, h, f * HS:(f + 1) * HS], k.xins[0:HS, h, f * P:(f + 1) * P],
                                            k.ident[0:HS, 0:HS])
                t.then_inc(k.s_xt, 1)

        @block.vector
        def _(dve):
            dve.wait_ge(k.s_const, 16 * 11)
            for q in range(8):
                pages = k.pages[:].rearrange("p (n q) -> p n q", q=8)[:, :, q]
                mine = k.pick[:, q:q + 1].broadcast_to([P, DB * LOADS])
                if q == 0:
                    nc.vector.tensor_tensor(k.idxf[:], pages, mine, ALU.mult).then_inc(k.s_idx, 1)
                else:
                    nc.vector.tensor_tensor(k.idxt[:], pages, mine, ALU.mult).then_inc(k.s_idx, 1)
                    dve.wait_ge(k.s_idx, 2 * q)
                    nc.vector.tensor_tensor(k.idxf[:], k.idxf[:], k.idxt[:], ALU.add).then_inc(k.s_idx, 1)
                    dve.wait_ge(k.s_idx, 2 * q + 1)
            nc.vector.tensor_scalar(k.idx[:], k.idxf[:], 16.0, k.row[:, 0:1], ALU.mult, ALU.add).then_inc(k.s_idx, 1)
            for u in range(8):
                dve.wait_ge(k.s_xt, u + 1)
                i, g = u // 2, u % 2
                nc.vector.tensor_copy(k.xT[:, 4 * g:4 * g + 4, i // 2, (i % 2) * P:(i % 2 + 1) * P],
                                      k.ps[:, u, :].rearrange("p (f n) -> p f n", f=4)).then_inc(k.s_xc, 1)
            for h in range(2):
                dve.wait_ge(k.s_xt, 9 + h)
                nc.vector.tensor_copy(k.xT[:, :, h, HP:HN],
                                      k.ps[:, h, 0:KD * HS].rearrange("p (f n) -> p f n", f=KD)).then_inc(k.s_xc, 1)


def nc_block(nc):
    def run(body):
        with nc.Block() as block:
            body(block)
    return run


A_UNITS = ([("pool", c, 0) for c in range(2)] + [("a", c, 1) for c in range(2)] + [("b", c, 2) for c in range(2)]
           + [("bg", c, 3) for c in range(2)] + [("cg", c, 4) for c in range(2)] + [("hh", c, 5) for c in range(2)]
           + [("qa", 0, 6), ("qa", 1, 6), ("kva", 0, 7), ("kr", 1, 7)])
A_WIDTH = [256] * 6 + [QL, KVL + ROPE]
A_COLUMN = [C_POOL, C_A, C_B, C_SC, C_SC + SCW, C_SC + 2 * SCW, C_QA, C_KV]
A_ROWS = {("qa", 1): QL - P, ("kr", 1): ROPE}


def project(k, l):
    nc, d, ps = k.nc, k.d, k.ps

    @nc_block(nc)
    def _(block):
        @block.sync
        def _(sp):
            one = bass.ds(l, 1)

            def projection(pos):
                w, c = A_WIDTH[pos], A_COLUMN[pos]
                fill(k, sp, pos, KD, w, rows(d["w_in"], l, KD)[:, :, c:c + w])

            for pos in range(SLOTS):
                projection(pos)
            for n, name in enumerate(("ln1_g", "ln1_b", "ln2_g", "ln2_b")):
                sp.dma_start(k.prm[:, 8 * n:8 * n + 8], d[name][one].rearrange("a (c p) -> p (a c)", p=P)).then_inc(k.s_prm2, 16)
            for t, r in ((0, P), (1, QL - P)):
                src = d["w_uq"][one, t * P:t * P + r, :].rearrange("a p (h n) -> p (a h) n", h=NH)
                sp.dma_start(k.wuqn[0:r, t].rearrange("p (h n) -> p h n", h=NH), src[:, :, 0:NOPE]).then_inc(k.s_prm2, 16)
                sp.dma_start(k.wuqr[0:r, t].rearrange("p (h n) -> p h n", h=NH), src[:, :, NOPE:NOPE + ROPE]).then_inc(k.s_prm2, 16)
            sp.dma_start(k.wuk[:], d["w_uk"][one].rearrange("a p h n -> (a p) (h n)")).then_inc(k.s_prm2, 16)
            for e in range(2):
                dst = k.wuv.rearrange("p (i e) n -> p e i n", e=2)[:, e, :, e * VH:(e + 1) * VH]
                src = d["w_uv"][one].rearrange("a p (i e) n -> (a p) e i n", e=2)[:, e]
                sp.dma_start(dst, src).then_inc(k.s_prm2, 16)
            for g in range(NG):
                o = 64 * (g % 2)
                sp.dma_start(k.poolw[o:o + 64, g // 2, o:o + 64], d["pool_w"][one, g].rearrange("a p n -> (a p) n")).then_inc(k.s_prm2, 16)
            sp.dma_start(k.router[:, :, 0:NG], rows(d["router_g"], l, KD)).then_inc(k.s_prm2, 16)
            sp.dma_start(k.router[:, :, NG:NG + NE], rows(d["router_e"], l, KD)).then_inc(k.s_prm2, 16)
            sp.dma_start(k.rbias[:, 0:NG], d["router_g_b"][one].broadcast_to([P, NG])).then_inc(k.s_prm2, 16)
            sp.dma_start(k.rbias[:, NG:NG + NE], d["router_e_b"][one].broadcast_to([P, NE])).then_inc(k.s_prm2, 16)
            sp.dma_start(d["new_pool_sample"][one, :, 0:POOLH - DS], d["state_pool"][one, :, DS:POOLH]).then_inc(k.s_kept, 16)
            sp.dma_start(d["new_conv_sample"][one, :, 0:CONVH - DS], d["state_conv"][one, :, DS:CONVH]).then_inc(k.s_kept, 16)
            for pos in range(SLOTS, 8):
                projection(pos)

        @block.scalar
        def _(act):
            one = bass.ds(l, 1)
            act.dma_start(k.hpool[0:120, :], d["state_pool"][one].rearrange("a b t c -> (a b t) c")).then_inc(k.s_hist, 16)
            for g in range(2):
                act.dma_start(k.hconv[0:120, g, :],
                              d["state_conv"][one, 4 * g:4 * g + 4].rearrange("a b t c -> (a b t) c")).then_inc(k.s_hist, 16)
            act.dma_start(k.hsc[0:16, :], d["state_sconv"][one].rearrange("a b t c -> (a b t) c")).then_inc(k.s_hist, 16)
            for n, (dst, name, pat) in enumerate((
                    (k.prm[:, 32:34], "pool_scale", "a (c p) -> p (a c)"), (k.prm[:, 34:36], "conv_b", "a (c p) -> p (a c)"),
                    (k.prm[:, 36:38], "conv_ln_g", "a (c p) -> p (a c)"), (k.prm[:, 38:40], "conv_ln_b", "a (c p) -> p (a c)"),
                    (k.prm[:, 42:43], "kv_norm_g", "a (c p) -> p (a c)"))):
                act.dma_start(dst, d[name][one].rearrange(pat, p=P)).then_inc(k.s_prm, 16)
            act.dma_start(k.prm[:, 40:41], d["q_norm_g"][one, 0:P].rearrange("a p -> p a")).then_inc(k.s_prm, 16)
            act.dma_start(k.prm[0:QL - P, 41:42], d["q_norm_g"][one, P:QL].rearrange("a p -> p a")).then_inc(k.s_prm, 16)
            for c in range(2):
                act.dma_start(k.cw[:, c, :], d["conv_w"][one, :, c * P:(c + 1) * P].rearrange("a k p -> p (a k)")).then_inc(k.s_prm, 16)
                act.dma_start(k.sw[:, c, :], d["sconv_w"][one, :, c * P:(c + 1) * P].rearrange("a k p -> p (a k)")).then_inc(k.s_prm, 16)

            def done(ins):
                ins.then_inc(k.a_evac, 1)

            act.wait_ge(k.a_mm, 1)
            act.wait_ge(k.a_zero, 3)
            nc.scalar.copy(k.up_s[:, :, :, 0:POOLH], ps[:, 0, 0:240].rearrange("p (c b t) -> p c b t", c=2, t=POOLH))
            nc.scalar.copy(k.v_s[:, :, :, 0:SCH], ps[:, 0, 240:272].rearrange("p (c b t) -> p c b t", c=2, t=SCH))
            done(nc.scalar.copy(k.glu_s[:, :, :, 0:CONVH], ps[:, 1, 0:480].rearrange("p (c b t) -> p c b t", c=2, t=CONVH)))
            for u, (name, c, pos) in enumerate(A_UNITS):
                n = u + 1
                act.wait_ge(k.a_mm, n + 1)
                m = A_ROWS.get((name, c), P)
                src = ps[0:m, 2 * (n % 4):2 * (n % 4) + 2, 0:HN]
                if name == "pool":
                    nc.scalar.copy(k.up_p[:, c, POOLH:POOLH + SEQ].rearrange("p (h n) -> p h n", h=2), prompt(src))
                    nc.scalar.copy(k.kcat[:, 0, c], src[:, :, HP:HN])
                    done(nc.scalar.copy(k.up_s[:, c].rearrange("p (h b) t -> p h b t", h=2)[:, :, :, POOLH:POOLH + DS], sample(src)))
                elif name == "b":
                    done(nc.scalar.activation(k.gb[:, c], src, ACT.Sigmoid))
                else:
                    dst = {"a": k.ga, "bg": k.dd, "cg": k.cg, "hh": k.hh, "qa": k.qa, "kva": k.kva, "kr": k.kr}[name]
                    done(nc.scalar.copy(dst[0:m, 0 if name == "kr" else c], src))
            act.wait_ge(k.a_mm, 18)
            nc.scalar.copy(k.tail[0:CONVH, 0:2, :], ps[0:CONVH, 2, 0:512].rearrange("p (s c) -> p s c", s=2))
            done(nc.scalar.copy(k.tail[0:SCH, 2, :], ps[0:SCH, 3, 0:256]))
            act.wait_ge(k.a_mm, 19)
            done(nc.scalar.copy(k.stail[0:HS, 0:2], ps[0:HS, 4:6, :].rearrange("p s (h c) -> p s h c", h=2)))
            act.wait_ge(k.a_mm, 20)
            done(nc.scalar.copy(k.stail[0:HS, 2], ps[0:HS, 6, :].rearrange("p (h c) -> p h c", h=2)))

        @block.gpsimd
        def _(pool):
            pool.memset(k.up_p[:, :, 0:POOLH], 0.0).then_inc(k.a_zero, 1)
            pool.memset(k.glu_p[:, :, 0:CONVH], 0.0).then_inc(k.a_zero, 1)
            pool.memset(k.v_p[:, :, 0:SCH], 0.0).then_inc(k.a_zero, 1)

        @block.tensor
        def _(pe):
            pe.wait_ge(k.s_hist, 64)
            for c in range(2):
                nc.tensor.transpose(ps[:, 0, c * 120:(c + 1) * 120], k.hpool[0:120, c * P:(c + 1) * P], k.ident[0:120, 0:120])
                nc.tensor.transpose(ps[:, 0, 240 + c * 16:256 + c * 16], k.hsc[0:16, c * P:(c + 1) * P], k.ident[0:16, 0:16])
                for g in range(2):
                    t = nc.tensor.transpose(ps[:, 1, c * 240 + g * 120:c * 240 + (g + 1) * 120],
                                            k.hconv[0:120, g, c * P:(c + 1) * P], k.ident[0:120, 0:120])
            t.then_inc(k.a_mm, 1)
            free = False
            for u, (name, c, pos) in enumerate(A_UNITS):
                n = u + 1
                if n >= 4:
                    pe.wait_ge(k.a_evac, n - 3)
                slot_ready(k, pe, pos)
                m = A_ROWS.get((name, c), P)
                w = slot(k, pos, KD, A_WIDTH[pos])
                for f in range(KD):
                    for h in range(2):
                        t = nc.tensor.matmul(ps[0:m, 2 * (n % 4) + h, 0:HN], w[:, f, c * P:c * P + m], k.xT[:, f, h, :],
                                             start=(f == 0), stop=(f == KD - 1))
                        if free:
                            t.then_inc(k.w_free, 1)
                            free = False
                t.then_inc(k.a_mm, 1)
                free = c == 1
            pe.wait_ge(k.a_done, 1)
            pe.wait_ge(k.a_evac, 14)
            for c in range(2):
                for s, (src, hist) in enumerate(((k.up_p, POOLH), (k.glu_p, CONVH))):
                    t = nc.tensor.transpose(ps[0:hist, 2, s * 256 + c * P:s * 256 + (c + 1) * P], src[:, c, SEQ:SEQ + hist], k.ident[:])
                    if free:
                        t.then_inc(k.w_free, 1)
                        free = False
                t = nc.tensor.transpose(ps[0:SCH, 3, c * P:(c + 1) * P], k.v_p[:, c, SEQ:SEQ + SCH], k.ident[:])
            t.then_inc(k.a_mm, 1)
            pe.wait_ge(k.a_evac, 15)
            for s in range(2):
                for h in range(2):
                    for c in range(2):
                        t = nc.tensor.transpose(ps[0:HS, 4 + s, h * 256 + c * P:h * 256 + (c + 1) * P], k.kcat[:, s, c, h, :], k.ident[:])
            t.then_inc(k.a_mm, 1)
            pe.wait_ge(k.a_evac, 16)
            for h in range(2):
                for c in range(2):
                    t = nc.tensor.transpose(ps[0:HS, 6, h * 256 + c * P:h * 256 + (c + 1) * P], k.kcat[:, 2, c, h, :], k.ident[:])
            t.then_inc(k.a_mm, 1)

        @block.vector
        def _(dve):
            ch = Chain(dve, k.a_chain)
            v = nc.vector
            dve.wait_ge(k.a_evac, 3)
            dve.wait_ge(k.a_zero, 3)
            for c in range(2):
                for src, sums, view, t in ((k.up_p[:, c], k.wp, prompt, POOLH + SEQ), (k.up_s[:, c], k.ws, sample, POOLH + DS)):
                    last, step, i = src, 1, 0
                    for _ in range((2, 4)[c]):
                        lo = 64 if (c, i) in ((0, 1), (1, 3)) else 0
                        out = sums[i % 2]
                        ch.settle()
                        o, a, b = (x[lo:P, ..., s:e] for x, s, e in ((out, 2 * step - 1, t), (last, 2 * step - 1, t), (last, step - 1, t - step)))
                        ch.step(v.tensor_tensor(o, a, b, ALU.add))
                        keep = {(0, 0): 0, (0, 1): 64, (1, 2): 0, (1, 3): 64}.get((c, i))
                        if keep is not None:
                            ch.settle()
                            r = slice(keep, keep + 64)
                            dst = view(k.pooled[r, c])
                            if view is prompt:
                                w = out[r, POOLH:t].rearrange("p (h n) -> p h n", h=2)
                                u = src[r, POOLH:t].rearrange("p (h n) -> p h n", h=2)
                            else:
                                w = out[r].rearrange("p (h b) t -> p h b t", h=2)[:, :, :, POOLH:t]
                                u = src[r].rearrange("p (h b) t -> p h b t", h=2)[:, :, :, POOLH:t]
                            ch.step(v.tensor_tensor(dst, w, view(k.pcnt[r, c]), ALU.mult))
                            ch.settle()
                            ch.step(v.tensor_tensor(dst, dst, u, ALU.subtract))
                        last, step, i = out, 2 * step, i + 1
            dve.wait_ge(k.a_evac, 7)
            for c in range(2):
                ch.step(v.tensor_tensor(k.glu_p[:, c, CONVH:].rearrange("p (h n) -> p h n", h=2), prompt(k.ga[:, c]), prompt(k.gb[:, c]), ALU.mult))
                ch.step(v.tensor_tensor(k.glu_s[:, c].rearrange("p (h b) t -> p h b t", h=2)[:, :, :, CONVH:], sample(k.ga[:, c]), sample(k.gb[:, c]), ALU.mult))
                ch.step(v.tensor_tensor(k.kcat[:, 1, c], k.ga[:, c, :, HP:HN], k.gb[:, c, :, HP:HN], ALU.mult))
            ch.settle()
            dve.wait_ge(k.s_prm, 16 * 11)

            def windows(src_p, src_s, c, tap):
                return (src_p[:, c, tap:tap + SEQ].rearrange("p (h n) -> p h n", h=2),
                        src_s[:, c].rearrange("p (h b) t -> p h b t", h=2)[:, :, :, tap:tap + DS])

            for tap in range(CONVK):
                for c in range(2):
                    for src, dst in zip(windows(k.glu_p, k.glu_s, c, tap), (prompt(k.y[:, c]), sample(k.y[:, c]))):
                        if tap == 0:
                            ch.step(v.tensor_scalar(dst, src, k.cw[:, c, 0:1], k.prm[:, 34 + c:35 + c], ALU.mult, ALU.add))
                        else:
                            ch.settle(3)
                            ch.step(v.scalar_tensor_tensor(dst, src, k.cw[:, c, tap:tap + 1], dst, ALU.mult, ALU.add))
            dve.wait_ge(k.a_evac, 13)
            for c in range(2):
                ch.step(v.tensor_tensor(k.v_p[:, c, SCH:].rearrange("p (h n) -> p h n", h=2), prompt(k.cg[:, c]), prompt(k.hh[:, c]), ALU.mult))
                ch.step(v.tensor_tensor(k.v_s[:, c].rearrange("p (h b) t -> p h b t", h=2)[:, :, :, SCH:], sample(k.cg[:, c]), sample(k.hh[:, c]), ALU.mult))
                ch.step(v.tensor_tensor(k.kcat[:, 2, c], k.cg[:, c, :, HP:HN], k.hh[:, c, :, HP:HN], ALU.mult))
            ch.settle()
            v.tensor_copy(k.stat[:, 0:1], k.prm[:, 32:33]).then_inc(k.a_done, 1)
            for tap in range(SCK):
                for c in range(2):
                    for src, dst in zip(windows(k.v_p, k.v_s, c, tap), (prompt(k.cv[:, c]), sample(k.cv[:, c]))):
                        if tap == 0:
                            ch.step(v.tensor_scalar(dst, src, k.sw[:, c, 0:1], None, ALU.mult))
                        else:
                            ch.settle(3)
                            ch.step(v.scalar_tensor_tensor(dst, src, k.sw[:, c, tap:tap + 1], dst, ALU.mult, ALU.add))
            ch.settle()
            v.tensor_tensor(k.dd[:], k.dd[:], k.cv[:], ALU.mult).then_inc(k.a_done, 1)


B_UNITS = (["krr:D", "kro:D", "wuk:A", "cmean:D", "qss:A", "kss:A", "cvar:A"] + [f"qn{i}:A" for i in range(4)]
           + ["qr0:D", "qr1:D", "rot0:D", "rot1:D"] + [f"ql{h}:A" for h in range(NH)]
           + ["mix0:A", "mix1:A", "ckvn:A", "krn:D", "qdr:D"])
B_AT = {name.split(":")[0]: n for n, name in enumerate(B_UNITS)}


def b_taken(engine, upto):
    return sum(name.endswith(engine) for name in B_UNITS[:upto])


def attend_inputs(k, l):
    nc, d, ps = k.nc, k.d, k.ps

    def bank(name):
        return ps[:, 2 * (B_AT[name] % 4):2 * (B_AT[name] % 4) + 2, :]

    def both(name, m=P):
        return bank(name)[0:m, :, 0:HN]

    @nc_block(nc)
    def _(block):
        @block.sync
        def _(sp):
            one = bass.ds(l, 1)
            sp.dma_start(d["new_pool_prompt"][one, 0].rearrange("a t c -> (a t) c"), k.tail[0:POOLH, 0, :]).then_inc(k.s_out, 16)
            sp.dma_start(d["new_conv_prompt"][one, 0].rearrange("a t c -> (a t) c"), k.tail[0:CONVH, 1, :]).then_inc(k.s_out, 16)
            sp.dma_start(d["new_sconv_prompt"][one, 0].rearrange("a t c -> (a t) c"), k.tail[0:SCH, 2, :]).then_inc(k.s_out, 16)
            for b in range(DB):
                h, r = b // 4, DS * (b % 4)
                for s, (out, a, z) in enumerate(((d["new_pool_sample"], POOLH - DS, POOLH), (d["new_conv_sample"], CONVH - DS, CONVH))):
                    sp.dma_start(out[one, b, a:z].rearrange("a t c -> (a t) c"), k.stail[r:r + DS, s, h, :]).then_inc(k.s_out, 16)
                sp.dma_start(d["new_sconv_sample"][one, b].rearrange("a t c -> (a t) c"), k.stail[r + DS - SCH:r + DS, 2, h, :]).then_inc(k.s_out, 16)
            sp.wait_ge(k.b_A, b_taken("A", B_AT["ckvn"] + 1))
            sp.wait_ge(k.b_D, b_taken("D", B_AT["krn"] + 1))
            for dst, full, part, w in ((d["new_ckv_prompt"], k.ckvn, None, KVL), (d["new_krope_prompt"], k.krn, None, ROPE)):
                for i in range(4):
                    sp.dma_start(dst[one, 0, i * P:(i + 1) * P].rearrange("a t c -> (a t) c"), full[:, i, :]).then_inc(k.s_out, 16)
            for dst, part in ((d["new_ckv_sample"], k.ckvs), (d["new_krope_sample"], k.krs)):
                for h in range(2):
                    sp.dma_start(dst[one, 4 * h:4 * h + 4].rearrange("a b t c -> (a b t) c"), part[0:HS, h, :]).then_inc(k.s_out, 16)

        @block.gpsimd
        def _(pool):
            pool.memset(k.wukT[:], 0.0).then_inc(k.b_zero, 1)
            pool.memset(k.krpad[:], 0.0).then_inc(k.b_zero, 1)
            pool.memset(k.qdr[:], 0.0).then_inc(k.b_zero, 1)
            for b in range(CACHES):
                load_cache(k, pool, b)

        @block.scalar
        def _(act):
            ch = Chain(act, k.b_chA)
            s = nc.scalar

            def take(name):
                act.wait_ge(k.b_mm, B_AT[name] + 1)

            def taken(ins):
                ins.then_inc(k.b_A, 1)

            s.activation(k.sqq[:, 0], k.qa[:, 0], ACT.Square)
            s.activation(k.sqq[0:QL - P, 1], k.qa[0:QL - P, 1], ACT.Square).then_inc(k.b_sq, 1)
            s.activation(k.sqk[:], k.kva[:, 0], ACT.Square).then_inc(k.b_sq, 1)
            take("wuk")
            act.wait_ge(k.b_zero, 1)
            w = bank("wuk")[:, 0, :].rearrange("p (i n) -> p i n", i=4)
            t = k.wukT.rearrange("p (i e) n -> p e i n", e=2)
            s.copy(t[0:64, 0], w[0:64])
            taken(s.copy(t[64:P, 1], w[64:P]))
            act.wait_ge(k.b_yc, 2)
            s.activation(k.sqc[:], k.yc[:], ACT.Square).then_inc(k.b_sq, 1)
            take("qss")
            taken(s.activation(k.rq[:], both("qss"), ACT.Sqrt, scale=1.0 / QL, bias=k.eps[:, 1:2]))
            take("kss")
            taken(s.activation(k.rk[:], both("kss"), ACT.Sqrt, scale=1.0 / KVL, bias=k.eps[:, 1:2]))
            take("cvar")
            taken(s.activation(k.rc[:], both("cvar"), ACT.Sqrt, scale=1.0 / CONVW, bias=k.eps[:, 0:1]))
            for i in range(4):
                take(f"qn{i}")
                taken(s.copy(k.qnope[:, i], both(f"qn{i}")))
            for h in range(NH):
                take(f"ql{h}")
                taken(s.copy(k.qlat[:, h], both(f"ql{h}")))
            for c in range(2):
                take(f"mix{c}")
                taken(s.activation(k.aa[:, c], both(f"mix{c}"), ACT.Identity, scale=k.prm[:, 32 + c:33 + c]))
            take("ckvn")
            s.copy(k.ckvn[:], bank("ckvn")[:, 0, :].rearrange("p (i n) -> p i n", i=4))
            taken(s.copy(k.ckvs[0:HS], bank("ckvn")[0:HS, 1, 0:256].rearrange("p (i n) -> p i n", i=2)))
            act.wait_ge(k.b_z, 1)
            for c in range(2):
                s.activation(k.bb[:, c], k.yc[:, c], ACT.Silu, scale=k.prm[:, 36 + c:37 + c], bias=k.prm[:, 38 + c:39 + c]).then_inc(k.b_sq, 1)

        @block.vector
        def _(dve):
            ch = Chain(dve, k.b_chD)
            v = nc.vector

            def take(name):
                dve.wait_ge(k.b_mm, B_AT[name] + 1)

            def taken(ins):
                ins.then_inc(k.b_D, 1)

            def flat(t):
                return t.rearrange("p (h n) -> p h n", h=2)

            take("krr")
            taken(v.tensor_tensor(k.t1[:], both("krr"), flat(k.cos), ALU.mult))
            take("kro")
            taken(v.tensor_tensor(k.t2[:], both("kro"), flat(k.sin), ALU.mult))
            dve.wait_ge(k.b_D, 2)
            dve.wait_ge(k.b_zero, 2)
            for j in range(4):
                r = slice(32 * j, 32 * j + 32)
                v.tensor_tensor(k.krpad[r, j], k.t1[r], k.t2[r], ALU.add).then_inc(k.b_kr, 1)
            take("cmean")
            for c in range(2):
                i = v.scalar_tensor_tensor(k.yc[:, c], both("cmean"), -1.0 / CONVW, k.y[:, c], ALU.mult, ALU.add)
                i.then_inc(k.b_yc, 1)
            dve.wait_ge(k.b_yc, 2)
            taken(v.tensor_copy(k.stat[:, 0:1], k.eps[:, 0:1]))
            dve.wait_ge(k.b_A, b_taken("A", B_AT["qss"] + 1))
            ch.step(v.reciprocal(k.rq[:], k.rq[:]))
            ch.settle()
            ch.step(v.scalar_tensor_tensor(k.qa[:, 0], k.qa[:, 0], k.prm[:, 40:41], k.rq[:], ALU.mult, ALU.mult))
            r = slice(0, QL - P)
            v.scalar_tensor_tensor(k.qa[r, 1], k.qa[r, 1], k.prm[r, 41:42], k.rq[r], ALU.mult, ALU.mult).then_inc(k.b_qn, 1)
            dve.wait_ge(k.b_A, b_taken("A", B_AT["kss"] + 1))
            ch.step(v.reciprocal(k.rk[:], k.rk[:]))
            ch.settle()
            v.scalar_tensor_tensor(k.ckvT[:], k.kva[:, 0], k.prm[:, 42:43], k.rk[:], ALU.mult, ALU.mult).then_inc(k.b_ckv, 1)
            dve.wait_ge(k.b_A, b_taken("A", B_AT["cvar"] + 1))
            ch.step(v.reciprocal(k.rc[:], k.rc[:]))
            ch.settle()
            for c in range(2):
                ch.step(v.tensor_tensor(k.yc[:, c], k.yc[:, c], k.rc[:], ALU.mult))
            ch.settle()
            v.tensor_copy(k.stat[:, 1:2], k.eps[:, 0:1]).then_inc(k.b_z, 1)
            for t in range(2):
                take(f"qr{t}")
                taken(v.tensor_copy(k.qr[:, t], both(f"qr{t}")))
            for t in range(2):
                take(f"rot{t}")
                ch.step(v.tensor_tensor(k.t1[:], k.qr[:, t], flat(k.cos), ALU.mult))
                taken(v.tensor_tensor(k.t2[:], both(f"rot{t}"), flat(k.sin), ALU.mult))
                ch.settle()
                dve.wait_ge(k.b_D, b_taken("D", B_AT[f"rot{t}"] + 1))
                v.tensor_tensor(k.qr[:, t], k.t1[:], k.t2[:], ALU.add).then_inc(k.b_qr, 1)
                dve.wait_ge(k.b_qr, t + 1)
            take("krn")
            v.tensor_copy(k.krn[:], bank("krn")[:, 0, 0:128].rearrange("p (i n) -> p i n", i=4)).then_inc(k.b_kr, 1)
            taken(v.tensor_copy(k.krs[0:HS], bank("krn")[0:HS, 1, 0:64].rearrange("p (i n) -> p i n", i=2)))
            take("qdr")
            dve.wait_ge(k.b_zero, 3)
            for j in range(4):
                r = slice(32 * j, 32 * j + 32)
                src = bank("qdr")[r, 0, 0:256].rearrange("p (h b t) -> p b h t", h=NH, b=DB)
                i = v.tensor_copy(k.qdr[r, :, j].rearrange("p b (h t) -> p b h t", h=NH), src)
            taken(i)

        @block.tensor
        def _(pe):
            m = nc.tensor

            def buffer(name):
                u = B_AT[name]
                if u >= 4:
                    engine = B_UNITS[u - 4][-1]
                    pe.wait_ge(k.b_A if engine == "A" else k.b_D, b_taken(engine, u - 3))

            def made(ins):
                ins.then_inc(k.b_mm, 1)

            def halves(name, terms, mrows=P):
                buffer(name)
                for h in range(2):
                    for n, (w, x) in enumerate(terms):
                        i = m.matmul(bank(name)[0:mrows, h, 0:HN], w, x[:, h], start=(n == 0), stop=(n == len(terms) - 1))
                made(i)

            pe.wait_ge(k.s_prm2, 16 * 19)
            halves("krr", [(k.sel[0:32, 0:P], k.kr[0:32, 0])])
            halves("kro", [(k.rotrep[0:32], k.kr[0:32, 0])])
            buffer("wuk")
            for i in range(4):
                t = m.transpose(bank("wuk")[:, 0, i * P:(i + 1) * P], k.wuk[:, i * P:(i + 1) * P], k.ident[:])
            made(t)
            halves("cmean", [(k.ones[:], k.y[:, c]) for c in range(2)])
            pe.wait_ge(k.b_sq, 2)
            halves("qss", [(k.ones[:], k.sqq[:, 0]), (k.ones[0:QL - P], k.sqq[0:QL - P, 1])])
            halves("kss", [(k.ones[:], k.sqk[:])])
            pe.wait_ge(k.b_sq, 3)
            halves("cvar", [(k.ones[:], k.sqc[:, c]) for c in range(2)])
            pe.wait_ge(k.b_qn, 1)
            for i in range(4):
                halves(f"qn{i}", [(k.wuqn[0:r, t, i * P:(i + 1) * P], k.qa[0:r, t]) for t, r in ((0, P), (1, QL - P))])
            for i in range(2):
                halves(f"qr{i}", [(k.wuqr[0:r, t, i * P:(i + 1) * P], k.qa[0:r, t]) for t, r in ((0, P), (1, QL - P))])
            for t in range(2):
                pe.wait_ge(k.b_D, b_taken("D", B_AT[f"qr{t}"] + 1))
                halves(f"rot{t}", [(k.rot[:], k.qr[:, t])])
            for h in range(NH):
                pe.wait_ge(k.b_A, b_taken("A", B_AT[f"qn{h // 2}"] + 1))
                halves(f"ql{h}", [(k.wukT[:, h, :], k.qnope[:, h // 2])])
            for c in range(2):
                halves(f"mix{c}", [(k.poolw[:, c, :], k.pooled[:, c])])
            buffer("ckvn")
            pe.wait_ge(k.b_ckv, 1)
            for i in range(4):
                m.transpose(bank("ckvn")[:, 0, i * P:(i + 1) * P], columns(k.ckvT, i // 2, i % 2), k.ident[:])
            for h in range(2):
                t = m.transpose(bank("ckvn")[0:HS, 1, h * P:(h + 1) * P], k.ckvT[:, h, HP:HN], k.ident[:])
            made(t)
            buffer("krn")
            pe.wait_ge(k.b_kr, 4)
            for i in range(4):
                m.transpose(bank("krn")[:, 0, i * 32:(i + 1) * 32], columns(k.krpad[0:32, 0], i // 2, i % 2), k.ident[0:32, 0:32])
            for h in range(2):
                t = m.transpose(bank("krn")[0:HS, 1, h * 32:(h + 1) * 32], k.krpad[0:32, 0, h, HP:HN], k.ident[0:32, 0:32])
            made(t)
            buffer("qdr")
            pe.wait_ge(k.b_qr, 2)
            for h in range(NH):
                t = m.matmul(bank("qdr")[:, 0, h * 32:(h + 1) * 32], k.sel[:, (h % 4) * P:(h % 4 + 1) * P],
                             k.qr[:, h // 4, :, HP:HN], start=True, stop=True)
            made(t)


PARTS = [(0, 4), (4, 6), (6, 8)]


def load_cache(k, pool, b, groups=range(GROUPS)):
    for n in range(groups[0] // 2, (groups[-1] + 1) // 2):
        s = (b % CACHES) * LOADS + n
        keys = k.ckv[:, b % CACHES, 2 * n:2 * n + 2].rearrange("p g n -> p (g n)")
        rotary = k.ckr[:, b % CACHES, 2 * n:2 * n + 2].rearrange("p g n -> p (g n)")
        for table, dst, landed in ((k.kr_table, rotary, k.c_inr[s]), (k.ckv_table, keys, k.c_in[s])):
            at = bass.IndirectOffsetOnAxis(ap=k.idx[:, b * LOADS + n:b * LOADS + n + 1], axis=0)
            pool.indirect_dma_start(dst, None, table, at).then_inc(landed, 16)


def attend_prompt(k, l):
    nc, ps = k.nc, k.ps
    STEPS = NH * 4

    @nc_block(nc)
    def _(block):
        @block.tensor
        def _(pe):
            m = nc.tensor
            for i in range(STEPS + 3):
                if i < STEPS:
                    h, qb = i // 4, i % 4
                    if i >= 4:
                        pe.wait_ge(k.c_exp, i - 3)
                    q = (columns(k.qlat[:, h], qb // 2, qb % 2), columns(k.qr[:, h // 4], qb // 2, qb % 2))
                    for kh in range(qb // 2 + 1):
                        w = min((qb + 1) * P - kh * HP, HP)
                        for n, (a, b) in enumerate(zip(q, (k.ckvT[:, kh, 0:w], k.krpad[:, h % 4, kh, 0:w]))):
                            t = m.matmul(ps[:, i % 4, kh * HP:kh * HP + w], a, b, start=(n == 0), stop=(n == 1))
                    t.then_inc(k.c_s, 1)
                j = i - 2
                if 0 <= j < STEPS:
                    pe.wait_ge(k.c_pn, j + 1)
                    if j >= 2:
                        pe.wait_ge(k.c_pt, j - 1)
                    for b in range(j % 4 + 1):
                        t = m.transpose(ps[:, 4 + j % 2, b * P:(b + 1) * P], k.prob[:, j % 3, b * P:(b + 1) * P], k.ident[:])
                    t.then_inc(k.c_t, 1)
                j = i - 3
                if 0 <= j < STEPS:
                    h, qb = j // 4, j % 4
                    pe.wait_ge(k.c_pt, j + 1)
                    if h >= 2 and qb == 0:
                        pe.wait_ge(k.c_lat, h - 1)
                    for b in range(qb + 1):
                        t = m.matmul(ps[:, 6 + h % 2, qb * P:(qb + 1) * P], k.ckvn[:, b, :], k.probT[:, j % 2, b * P:(b + 1) * P],
                                     start=(b == 0), stop=(b == qb))
                    t.then_inc(k.c_v, 1)

        @block.vector
        def _(dve):
            ch = Chain(dve, k.c_chain)
            v = nc.vector

            def head_out(h):
                dve.wait_ge(k.c_v, 4 * h + 4)
                v.tensor_copy(prompt(k.lat[:, h]), ps[:, 6 + h % 2, :].rearrange("p (h n) -> p h n", h=2)).then_inc(k.c_lat, 1)

            for i in range(STEPS + 1):
                if i < STEPS:
                    qb = i % 4
                    w = (qb + 1) * P
                    dve.wait_ge(k.c_s, i + 1)
                    s = ps[:, i % 4, :]
                    ch.step(v.tensor_tensor(s[:, w - P:w], s[:, w - P:w], k.cmask[:], ALU.add))
                    ch.settle()
                    ch.step(v.reduce_max(k.mx[:, i:i + 1], s[:, 0:w], AX.X))
                    ch.settle()
                    v.tensor_scalar(k.nm[:, i:i + 1], k.mx[:, i:i + 1], -SCALE, None, ALU.mult).then_inc(k.c_m, 1)
                j = i - 1
                if j >= 0:
                    dve.wait_ge(k.c_exp, j + 1)
                    ch.step(v.reciprocal(k.rs[:, j:j + 1], k.sm[:, j:j + 1]))
                    ch.settle()
                    p = k.prob[:, j % 3, 0:(j % 4 + 1) * P]
                    v.tensor_scalar(p, p, k.rs[:, j:j + 1], None, ALU.mult).then_inc(k.c_pn, 1)
                if i % 4 == 3 and i >= 7:
                    head_out(i // 4 - 1)
            head_out(NH - 1)

        @block.scalar
        def _(act):
            for i in range(STEPS + 2):
                if i < STEPS:
                    w = (i % 4 + 1) * P
                    act.wait_ge(k.c_m, i + 1)
                    if i >= 3:
                        act.wait_ge(k.c_t, i - 2)
                    nc.scalar.activation(k.prob[:, i % 3, 0:w], ps[:, i % 4, 0:w], ACT.Exp, bias=k.nm[:, i:i + 1], scale=SCALE,
                                         accum_out=k.sm[:, i:i + 1]).then_inc(k.c_exp, 1)
                j = i - 2
                if j >= 0:
                    w = (j % 4 + 1) * P
                    act.wait_ge(k.c_t, j + 1)
                    if j >= 2:
                        act.wait_ge(k.c_v, j - 1)
                    nc.scalar.copy(k.probT[:, j % 2, 0:w], ps[:, 4 + j % 2, 0:w]).then_inc(k.c_pt, 1)


def attend_sample(k, l):
    nc, ps = k.nc, k.ps
    TOTAL = DB * GROUPS
    MISC, LAT = 7, 6

    @nc_block(nc)
    def _(block):
        @block.gpsimd
        def _(pool):
            for b in range(CACHES, DB):
                for n, (lo, hi) in enumerate(PARTS):
                    pool.wait_ge(k.d_pv, 3 * (b - CACHES) + n + 1)
                    load_cache(k, pool, b, range(lo, hi))

        @block.tensor
        def _(pe):
            m = nc.tensor
            for h in range(2):
                for n in range(NH):
                    out = ps[0:HS, MISC, (h * NH + n) * HS:(h * NH + n + 1) * HS]
                    m.matmul(out, k.ckvT[:, h, HP:HN], k.qlat[:, n, h, HP:HN], start=True, stop=False)
                    t = m.matmul(out, k.krpad[:, n % 4, h, HP:HN], k.qr[:, n // 4, h, HP:HN], start=False, stop=True)
            t.then_inc(k.d_sn, 1)

            def turn(n):
                b, g = n // GROUPS, n % GROUPS
                if g % 4 == 0:
                    u = n // 4
                    if u >= 1:
                        pe.wait_ge(k.d_krc, u)
                    for j in range(4):
                        if j % 2 == 0:
                            pe.wait_ge(k.c_inr[(b % CACHES) * LOADS + (g + j) // 2], 16 * (b // CACHES + 1))
                        t = m.transpose(ps[:, 5, j * P:(j + 1) * P], k.ckr[:, b % CACHES, g + j, :], k.ident[:])
                    t.then_inc(k.d_krt, 1)
                if g % 2 == 0:
                    pe.wait_ge(k.c_in[(b % CACHES) * LOADS + g // 2], 16 * (b // CACHES + 1))
                if n >= 2:
                    pe.wait_ge(k.d_kc, n - 1)
                for j in range(4):
                    t = m.transpose(ps[:, 3 + n % 2, j * P:(j + 1) * P], k.ckv[:, b % CACHES, g, j * P:(j + 1) * P], k.ident[:])
                t.then_inc(k.d_kt, 1)

            def scores(n):
                b, g = n // GROUPS, n % GROUPS
                u = n // 4
                pe.wait_ge(k.d_kc, n + 1)
                if g % 4 == 0:
                    pe.wait_ge(k.d_krc, u + 1)
                    if u >= 3:
                        pe.wait_ge(k.d_sub, u - 2)
                q = k.qlat[:, :, b // 4, HP + DS * (b % 4):HP + DS * (b % 4) + DS]
                c = (g % 4) * P
                m.matmul(ps[:, u % 3, c:c + P], k.krT[:, u % 2, c:c + P], k.qdr[:, b].rearrange("p j q -> p (j q)"),
                         start=True, stop=False, skip_group_check=True)
                for j in range(4):
                    t = m.matmul(ps[:, u % 3, c + 32 * j:c + 32 * j + 32], k.kT[:, n % 2, j * P:(j + 1) * P], q,
                                 start=False, stop=(j == 3), skip_group_check=True)
                t.then_inc(k.d_s, 1)

            def max_turn(b):
                pe.wait_ge(k.d_m1, b + 1)
                m.transpose(ps[0:32, MISC, 0:P], k.m1[:, :], k.ident[:]).then_inc(k.d_mt, 1)

            def max_spread(b):
                pe.wait_ge(k.d_dg, b + 1)
                m.matmul(ps[:, MISC, 0:32], k.ones[0:32, :], k.dg[0:32, :], start=True, stop=True).then_inc(k.d_mb, 1)

            def sum_spread(b):
                pe.wait_ge(k.d_ss, b + 1)
                m.matmul(ps[:, MISC, 0:32], k.ones[:], k.ss[:], start=True, stop=True).then_inc(k.d_sd, 1)

            def values(b, part):
                lo, hi = 4 * part[0], 4 * part[1]
                if lo == 0:
                    pe.wait_ge(k.d_exp, 3 * b + 3)
                    if b >= 1:
                        pe.wait_ge(k.d_lat, b)
                for t in range(lo, hi):
                    i = m.matmul(ps[:, LAT, 0:32], k.ckv[:, b % CACHES, t // 4, (t % 4) * P:(t % 4 + 1) * P],
                                 k.pd[:, b % 2, t * 32:(t + 1) * 32], start=(t == 0), stop=False)
                if part[1] == GROUPS:
                    i = m.matmul(ps[:, LAT, 0:32], k.ckvs[0:HS, b // 4, :], k.pn[0:HS, b % 2, :], start=False, stop=True)
                i.then_inc(k.d_pv, 1)

            turn(0)
            for n in range(TOTAL):
                b, g = n // GROUPS, n % GROUPS
                if n + 1 < TOTAL:
                    turn(n + 1)
                scores(n)
                if b >= 1:
                    if g == 2:
                        max_turn(b - 1)
                    if g == 3:
                        max_spread(b - 1)
                    if 4 <= g < 7:
                        values(b - 1, PARTS[g - 4])
                    if g == 7:
                        sum_spread(b - 1)
            max_turn(DB - 1)
            max_spread(DB - 1)
            for part in PARTS:
                values(DB - 1, part)
            sum_spread(DB - 1)

        @block.scalar
        def _(act):
            s = nc.scalar

            def probs(b):
                for i in range(2):
                    act.wait_ge(k.d_sub, 2 * b + i + 1)
                    p = k.pd[:, b % 2, i * 512:(i + 1) * 512]
                    s.activation(p, p, ACT.Exp, scale=SCALE).then_inc(k.d_exp, 1)
                act.wait_ge(k.d_pn, b + 1)
                p = k.pn[0:HS, b % 2, :]
                s.activation(p, p, ACT.Exp, scale=SCALE).then_inc(k.d_exp, 1)

            for n in range(TOTAL):
                b, g, u = n // GROUPS, n % GROUPS, n // 4
                if g % 4 == 0:
                    act.wait_ge(k.d_krt, u + 1)
                    if u >= 2:
                        act.wait_ge(k.d_s, 4 * (u - 1))
                    s.copy(k.krT[:, u % 2, :], ps[:, 5, :]).then_inc(k.d_krc, 1)
                act.wait_ge(k.d_kt, n + 1)
                if n >= 2:
                    act.wait_ge(k.d_s, n - 1)
                s.copy(k.kT[:, n % 2, :], ps[:, 3 + n % 2, :]).then_inc(k.d_kc, 1)
                if b >= 1 and g == 4:
                    probs(b - 1)
            probs(DB - 1)

        @block.vector
        def _(dve):
            ch = Chain(dve, k.d_chain)
            v = nc.vector
            dve.wait_ge(k.d_sn, 1)
            src = ps[0:HS, MISC, 0:256].rearrange("p (h n b t) -> p h b n t", h=2, n=NH, t=DS)
            for h in range(2):
                dst = k.sn[0:HS, 4 * h:4 * h + 4].rearrange("p b (n t) -> p b n t", n=NH)
                msk = k.nmask[0:HS, 4 * h:4 * h + 4].rearrange("p b (n t) -> p b n t", n=NH)
                ch.step(v.tensor_tensor(dst, src[:, h], msk, ALU.add))
            for b in range(DB):
                for i in range(2):
                    u = 2 * b + i
                    dve.wait_ge(k.d_s, 4 * u + 4)
                    ch.step(v.tensor_reduce(k.mab[:, i, :], ps[:, u % 3, :].rearrange("p (t q) -> p q t", q=32), AX.X, ALU.max))
                ch.settle()
                ch.step(v.tensor_tensor(k.m1[:], k.mab[:, 0, :], k.mab[:, 1, :], ALU.max))
                ch.settle()
                v.tensor_tensor(k.m1[0:HS], k.m1[0:HS], k.sn[0:HS, b, :], ALU.max).then_inc(k.d_m1, 1)
                dve.wait_ge(k.d_mt, b + 1)
                ch.step(v.reduce_max(k.stat[0:32, 0:1], ps[0:32, MISC, 0:P], AX.X))
                ch.settle()
                v.tensor_scalar(k.dg[0:32, :], k.ident[0:32, 0:32], k.stat[0:32, 0:1], None, ALU.mult).then_inc(k.d_dg, 1)
                dve.wait_ge(k.d_mb, b + 1)
                ch.step(v.tensor_copy(k.mb[:], ps[:, MISC, 0:32]))
                ch.settle()
                if b >= 2:
                    dve.wait_ge(k.d_pv, 3 * (b - 1))
                for i in range(2):
                    u = 2 * b + i
                    v.tensor_tensor(k.pd[:, b % 2, i * 512:(i + 1) * 512].rearrange("p (t q) -> p t q", q=32),
                                    ps[:, u % 3, :].rearrange("p (t q) -> p t q", q=32),
                                    k.mb[:, None, :].broadcast_to([P, 16, 32]), ALU.subtract).then_inc(k.d_sub, 1)
                v.tensor_tensor(k.pn[0:HS, b % 2, :], k.sn[0:HS, b, :], k.mb[0:HS], ALU.subtract).then_inc(k.d_pn, 1)
                dve.wait_ge(k.d_exp, 3 * b + 3)
                ch.step(v.tensor_reduce(k.ss[:], k.pd[:, b % 2, :].rearrange("p (t q) -> p q t", q=32), AX.X, ALU.add))
                ch.settle()
                v.tensor_tensor(k.ss[0:HS], k.ss[0:HS], k.pn[0:HS, b % 2, :], ALU.add).then_inc(k.d_ss, 1)
                dve.wait_ge(k.d_sd, b + 1)
                ch.step(v.reciprocal(k.ri[:], ps[:, MISC, 0:32]))
                ch.settle()
                dve.wait_ge(k.d_pv, 3 * (b + 1))
                c = HP + DS * (b % 4)
                v.tensor_tensor(k.lat[:, :, b // 4, c:c + DS], ps[:, LAT, 0:32].rearrange("p (h t) -> p h t", t=DS),
                                k.ri[:].rearrange("p (h t) -> p h t", t=DS), ALU.mult).then_inc(k.d_lat, 1)


BRANCH_TILES = [2, 2, 4, 2]


def merge(k, l):
    nc, d, ps = k.nc, k.d, k.ps
    units = [(mp, b, mi) for mp in range(4) for b in range(NB) for mi in range(2)]

    def pair(buffer):
        return ps[:, 2 * buffer:2 * buffer + 2, 0:HN]

    @nc_block(nc)
    def _(block):
        @block.sync
        def _(sp):
            pos = POS_BRANCH
            for mp in range(4):
                for b, p in enumerate((d["p_pool"], d["p_conv"], d["p_attn"], d["p_sconv"])):
                    fill(k, sp, pos, BRANCH_TILES[b], 256, rows(p, l, BRANCH_TILES[b])[:, :, 256 * mp:256 * mp + 256])
                    c = C_GATE + b * D + 256 * mp
                    fill(k, sp, pos + 1, KD, 256, rows(d["w_in"], l, KD)[:, :, c:c + 256])
                    pos += 2
            for i in range(4):
                fill(k, sp, POS_WO + i, KD, 256, rows(d["w_o"], l, KD)[:, :, 256 * i:256 * i + 256])

        @block.tensor
        def _(pe):
            m = nc.tensor
            for i in range(4):
                for h in range(2):
                    for e in range(2):
                        t = m.matmul(ps[:, 2 * i + h, 0:HN], k.wuv[:, 2 * i + e, :], k.lat[:, 2 * i + e, h, :], start=(e == 0), stop=(e == 1))
                t.then_inc(k.e_cm, 1)
            pe.wait_ge(k.e_c, 4)
            branches = (k.aa, k.bb, k.cc, k.dd)
            free = 0
            for n, (mp, b, mi) in enumerate(units):
                pos = POS_BRANCH + 2 * (NB * mp + b)
                if mi == 0:
                    slot_ready(k, pe, pos)
                    slot_ready(k, pe, pos + 1)
                if n >= 2:
                    pe.wait_ge(k.e_sg, n - 1)
                w = slot(k, pos + 1, KD, 256)
                for f in range(KD):
                    for h in range(2):
                        t = m.matmul(ps[:, 4 * (n % 2) + h, 0:HN], w[:, f, mi * P:(mi + 1) * P], k.xT[:, f, h, :],
                                     start=(f == 0), stop=(f == KD - 1))
                        if free:
                            t.then_inc(k.w_free, free)
                            free = 0
                t.then_inc(k.e_g, 1)
                if n >= 2:
                    pe.wait_ge(k.e_mg, n - 1)
                w = slot(k, pos, BRANCH_TILES[b], 256)
                for f in range(BRANCH_TILES[b]):
                    for h in range(2):
                        t = m.matmul(ps[:, 4 * (n % 2) + 2 + h, 0:HN], w[:, f, mi * P:(mi + 1) * P], branches[b][:, f, h, :],
                                     start=(f == 0), stop=(f == BRANCH_TILES[b] - 1))
                t.then_inc(k.e_p, 1)
                free = 2 * mi
            pe.wait_ge(k.e_mg, len(units))
            for o in range(KD):
                pos = POS_WO + o // 2
                slot_ready(k, pe, pos)
                if o >= 4:
                    pe.wait_ge(k.e_z, o - 3)
                w = slot(k, pos, KD, 256)
                for f in range(KD):
                    for h in range(2):
                        t = m.matmul(ps[:, 2 * (o % 4) + h, 0:HN], w[:, f, (o % 2) * P:(o % 2 + 1) * P], k.merged[:, f, h, :],
                                     start=(f == 0), stop=(f == KD - 1))
                        if free:
                            t.then_inc(k.w_free, free)
                            free = 0
                t.then_inc(k.e_o, 1)
                free = o % 2

        @block.scalar
        def _(act):
            for i in range(4):
                act.wait_ge(k.e_cm, i + 1)
                nc.scalar.copy(k.cc[:, i], pair(i)).then_inc(k.e_c, 1)
            for n in range(len(units)):
                act.wait_ge(k.e_g, n + 1)
                if n >= 2:
                    act.wait_ge(k.e_mg, n - 1)
                nc.scalar.activation(k.sg[:, n % 2], pair(2 * (n % 2)), ACT.Sigmoid).then_inc(k.e_sg, 1)

        @block.vector
        def _(dve):
            v = nc.vector
            for n, (mp, b, mi) in enumerate(units):
                dve.wait_ge(k.e_sg, n + 1)
                dve.wait_ge(k.e_p, n + 1)
                out = k.merged[:, 2 * mp + mi]
                g, p = k.sg[:, n % 2], pair(2 * (n % 2) + 1)
                if b == 0:
                    v.tensor_tensor(out, g, p, ALU.mult).then_inc(k.e_mg, 1)
                else:
                    v.tensor_tensor(g, g, p, ALU.mult).then_inc(k.e_t, 1)
                    dve.wait_ge(k.e_t, n - 2 * mp - 1)
                    v.tensor_tensor(out, out, g, ALU.add).then_inc(k.e_mg, 1)
            for o in range(KD):
                dve.wait_ge(k.e_o, o + 1)
                v.scalar_tensor_tensor(k.xT[:, o], k.xT[:, o], ALPHA, pair(o % 4), ALU.mult, ALU.add).then_inc(k.e_z, 1)


def layer_norm(k, s, gain, bias):
    nc, ps = k.nc, k.ps

    @nc_block(nc)
    def _(block):
        @block.tensor
        def _(pe):
            for f in range(KD):
                for h in range(2):
                    t = nc.tensor.matmul(ps[:, h, 0:HN], k.ones[:], k.xT[:, f, h, :], start=(f == 0), stop=(f == KD - 1))
            t.then_inc(s.mean, 1)
            for f in range(KD):
                pe.wait_ge(s.sq, f + 1)
                for h in range(2):
                    t = nc.tensor.matmul(ps[:, 2 + h, 0:HN], k.ones[:], k.sq[:, f % 2, h, :], start=(f == 0), stop=(f == KD - 1))
                t.then_inc(s.var, 1)

        @block.vector
        def _(dve):
            v = nc.vector
            dve.wait_ge(s.mean, 1)
            for f in range(KD):
                v.scalar_tensor_tensor(k.xT[:, f], ps[:, 0:2, 0:HN], -1.0 / D, k.xT[:, f], ALU.mult, ALU.add).then_inc(s.c, 1)
            dve.wait_ge(s.sd, 1)
            v.reciprocal(k.sd[:], k.sd[:]).then_inc(s.r, 1)
            dve.wait_ge(s.r, 1)
            for f in range(KD):
                v.tensor_tensor(k.xT[:, f], k.xT[:, f], k.sd[:], ALU.mult).then_inc(s.n, 1)

        @block.scalar
        def _(act):
            for f in range(KD):
                act.wait_ge(s.c, f + 1)
                if f >= 2:
                    act.wait_ge(s.var, f - 1)
                nc.scalar.activation(k.sq[:, f % 2], k.xT[:, f], ACT.Square).then_inc(s.sq, 1)
            act.wait_ge(s.var, KD)
            nc.scalar.activation(k.sd[:], ps[:, 2:4, 0:HN], ACT.Sqrt, scale=1.0 / D, bias=k.eps[:, 0:1]).then_inc(s.sd, 1)
            for f in range(KD):
                act.wait_ge(s.n, f + 1)
                nc.scalar.activation(k.xT[:, f], k.xT[:, f], ACT.Identity, scale=k.prm[:, gain + f:gain + f + 1],
                                     bias=k.prm[:, bias + f:bias + f + 1]).then_inc(s.x, 1)


def experts(k, l):
    nc, d, ps = k.nc, k.d, k.ps
    UNITS = NE * 4
    tiles = [(i * P, min(P, N - i * P)) for i in range(5)]
    flat = k.xT.rearrange("p f h n -> p f (h n)")

    @nc_block(nc)
    def _(block):
        @block.sync
        def _(sp):
            for e in range(NE):
                for i, w in enumerate((d["exp_w_gate"], d["exp_w_up"])):
                    src = w[bass.ds(l, 1), e].rearrange("a (k p) n -> p (a k) n", k=KD)
                    fill(k, sp, POS_EXPERT + 2 * e + i, KD, FF, src)
            for o in range(KD):
                src = d["exp_w_down"][bass.ds(l, 1)].rearrange("a e (j p) n -> p (a e j) n", j=2)
                for i in range(2):
                    fill(k, sp, POS_DOWN + 2 * o + i, 16, P, src[:, 16 * i:16 * i + 16, o * P:(o + 1) * P])

        @block.tensor
        def _(pe):
            m = nc.tensor
            for i, (c, r) in enumerate(tiles):
                for f in range(KD):
                    t = m.matmul(ps[0:r, 6, i * 20:(i + 1) * 20], flat[:, f, c:c + r], k.router[:, f, :], start=(f == 0), stop=(f == KD - 1))
            t.then_inc(k.f_lg, 1)
            free = 1

            def unit(n):
                nonlocal free
                e, j, h = n // 4, n // 2 % 2, n % 2
                pos = POS_EXPERT + 2 * e
                if n % 4 == 0:
                    slot_ready(k, pe, pos)
                    slot_ready(k, pe, pos + 1)
                if n >= 3:
                    pe.wait_ge(k.f_h, n - 2)
                for i in range(2):
                    w = slot(k, pos + i, KD, FF)
                    for f in range(KD):
                        t = m.matmul(ps[:, 2 * (n % 3) + i, 0:HN], w[:, f, j * P:(j + 1) * P], k.xT[:, f, h, :],
                                     start=(f == 0), stop=(f == KD - 1))
                        if free:
                            t.then_inc(k.w_free, free)
                            free = 0
                t.then_inc(k.f_u, 1)
                if n % 4 == 3:
                    free = 2

            def weights(e):
                if e >= 1:
                    pe.wait_ge(k.f_h, 4 * e)
                for h in range(2):
                    t = m.matmul(ps[:, 6 + h, 0:HN], k.ident[0:NE, e:e + 1].broadcast_to([NE, P]), k.combT[0:NE, h * HN:(h + 1) * HN],
                                 start=True, stop=True)
                t.then_inc(k.f_w, 1)

            for n in range(UNITS):
                unit(n)
                if n == 2:
                    pe.wait_ge(k.f_cb, 1)
                    for i, (c, r) in enumerate(tiles):
                        t = m.transpose(ps[0:NE, 6 + i // 4, (i % 4) * P:(i % 4) * P + r], k.comb[0:r, i, :], k.ident[0:r, 0:r])
                    t.then_inc(k.f_ct, 1)
                    pe.wait_ge(k.f_cc, 2)
                    weights(0)
                elif n >= 4 and n % 4 == 0:
                    weights(n // 4)
            pe.wait_ge(k.f_h, UNITS)
            for o in range(KD):
                if o >= 3:
                    pe.wait_ge(k.f_z, o - 2)
                for i in range(2):
                    pos = POS_DOWN + 2 * o + i
                    slot_ready(k, pe, pos)
                    w = slot(k, pos, 16, P)
                    for f in range(16):
                        for h in range(2):
                            t = m.matmul(ps[:, 2 * (o % 3) + h, 0:HN], w[:, f, :], k.hid[:, 16 * i + f, h, :],
                                         start=(i == 0 and f == 0), stop=(i == 1 and f == 15))
                            if free:
                                t.then_inc(k.w_free, free)
                                free = 0
                    free = 1
                t.then_inc(k.f_d, 1)

        @block.scalar
        def _(act):
            s = nc.scalar
            act.wait_ge(k.f_r, 1)
            s.activation(k.ge[:], k.ge[:], ACT.Exp).then_inc(k.f_ra, 1)
            act.wait_ge(k.f_r, 2)
            s.activation(k.e2[:], k.e2[:], ACT.Exp).then_inc(k.f_ra, 1)
            act.wait_ge(k.f_ct, 1)
            s.copy(k.combT[0:NE, 0:512], ps[0:NE, 6, :]).then_inc(k.f_cc, 1)
            s.copy(k.combT[0:NE, 512:N], ps[0:NE, 7, 0:32]).then_inc(k.f_cc, 1)
            for n in range(UNITS):
                act.wait_ge(k.f_u, n + 1)
                if n >= 3:
                    act.wait_ge(k.f_h, n - 2)
                s.activation(k.sgf[:, n % 3], ps[:, 2 * (n % 3), 0:HN], ACT.Silu).then_inc(k.f_sg, 1)

        @block.vector
        def _(dve):
            ch = Chain(dve, k.f_chain)
            v = nc.vector

            def step(ins):
                ch.step(ins)
                ch.settle()

            def spread(t, shape):
                return t[:, :, None].broadcast_to(shape)

            T5 = [P, 5, 4]
            step(v.memset(k.lg[:], 0.0))
            dve.wait_ge(k.f_lg, 1)
            step(v.tensor_copy(k.lg[:, 0:4], ps[:, 6, 0:80].rearrange("p (i c) -> p i c", c=20)))
            step(v.tensor_copy(k.lg[0:32, 4], ps[0:32, 6, 80:100]))
            step(v.tensor_tensor(k.lg[:], k.lg[:], k.rbias[:, None, :].broadcast_to([P, 5, 20]), ALU.add))
            gl = k.lg[:, :, 0:NG]
            step(v.tensor_reduce(k.gm[:], gl, AX.X, ALU.max))
            step(v.tensor_tensor(k.g1[:], gl, spread(k.gm, T5), ALU.is_equal))
            step(v.tensor_tensor(k.g1[:], k.g1[:], k.rank[:, None, :].broadcast_to(T5), ALU.mult))
            step(v.tensor_reduce(k.r1[:], k.g1[:], AX.X, ALU.max))
            step(v.tensor_tensor(k.g1[:], k.g1[:], spread(k.r1, T5), ALU.is_equal))
            v.tensor_tensor(k.ge[:], gl, spread(k.gm, T5), ALU.subtract).then_inc(k.f_r, 1)
            dve.wait_ge(k.f_ra, 1)
            step(v.tensor_reduce(k.gw[:], k.ge[:], AX.X, ALU.add))
            step(v.reciprocal(k.gw[:], k.gw[:]))
            el = k.lg[:, :, NG:NG + NE]
            for g in range(NG):
                x = el[:, :, 4 * g:4 * g + 4]
                oh = k.g1[:, :, g:g + 1].broadcast_to(T5)
                if g == 0:
                    step(v.tensor_tensor(k.es[:], x, oh, ALU.mult))
                else:
                    step(v.tensor_tensor(k.tt[:], x, oh, ALU.mult))
                    step(v.tensor_tensor(k.es[:], k.es[:], k.tt[:], ALU.add))

            def first(best, hot):
                step(v.tensor_reduce(best[:], k.es[:], AX.X, ALU.max))
                step(v.tensor_tensor(hot[:], k.es[:], spread(best, T5), ALU.is_equal))
                step(v.tensor_tensor(hot[:], hot[:], k.rank[:, None, :].broadcast_to(T5), ALU.mult))
                step(v.tensor_reduce(k.r1[:], hot[:], AX.X, ALU.max))
                step(v.tensor_tensor(hot[:], hot[:], spread(k.r1, T5), ALU.is_equal))

            first(k.b1, k.o1)
            step(v.scalar_tensor_tensor(k.es[:], k.o1[:], NEG, k.es[:], ALU.mult, ALU.add))
            first(k.b2, k.o2)
            v.tensor_tensor(k.e2[:], k.b2[:], k.b1[:], ALU.subtract).then_inc(k.f_r, 1)
            dve.wait_ge(k.f_ra, 2)
            step(v.tensor_scalar(k.b1[:], k.e2[:], 1.0, None, ALU.add))
            step(v.reciprocal(k.b1[:], k.b1[:]))
            step(v.tensor_tensor(k.b1[:], k.b1[:], k.gw[:], ALU.mult))
            step(v.tensor_tensor(k.b2[:], k.b1[:], k.e2[:], ALU.mult))
            step(v.tensor_tensor(k.o1[:], k.o1[:], spread(k.b1, T5), ALU.mult))
            step(v.tensor_tensor(k.o2[:], k.o2[:], spread(k.b2, T5), ALU.mult))
            step(v.tensor_tensor(k.o1[:], k.o1[:], k.o2[:], ALU.add))
            for g in range(NG):
                i = v.tensor_tensor(k.comb[:, :, 4 * g:4 * g + 4], k.o1[:], k.g1[:, :, g:g + 1].broadcast_to(T5), ALU.mult)
            i.then_inc(k.f_cb, 1)

            for n in range(UNITS):
                e, j, h = n // 4, n // 2 % 2, n % 2
                dve.wait_ge(k.f_sg, n + 1)
                if n % 4 == 0:
                    dve.wait_ge(k.f_w, e + 1)
                v.tensor_tensor(k.sgf[:, n % 3], k.sgf[:, n % 3], ps[:, 6 + h, 0:HN], ALU.mult).then_inc(k.f_t, 1)
                dve.wait_ge(k.f_t, n + 1)
                v.tensor_tensor(k.hid[:, 2 * e + j, h, :], k.sgf[:, n % 3], ps[:, 2 * (n % 3) + 1, 0:HN], ALU.mult).then_inc(k.f_h, 1)
            for o in range(KD):
                dve.wait_ge(k.f_d, o + 1)
                v.scalar_tensor_tensor(k.xT[:, o], k.xT[:, o], ALPHA, ps[:, 2 * (o % 3):2 * (o % 3) + 2, 0:HN], ALU.mult, ALU.add).then_inc(k.f_z, 1)


def end_layer(k):
    nc = k.nc

    @nc_block(nc)
    def _(block):
        @block.vector
        def _(dve):
            rows_per_layer = float(k.n_pool * PAGE // 8)
            nc.vector.tensor_scalar(k.idx[:], k.idx[:], rows_per_layer, None, ALU.add).then_inc(k.s_idx, 1)

        @block.gpsimd
        def _(pool):
            for i in range(CACHES * LOADS):
                for s in (k.c_in[i], k.c_inr[i]):
                    pool.wait_ge(s, 16 * len(range(i // LOADS, DB, CACHES)))

        @block.sync
        def _(sp):
            sp.wait_ge(k.s_out, 16 * (3 + 3 * DB + 8 + 4))
            sp.wait_ge(k.s_kept, 32)

    nc.all_engine_barrier()
    first = k.c_in[0].num
    caches = range(first, first + len(k.c_in + k.c_inr))
    nc.gpsimd.dma_reset(caches)
    nc.gpsimd.sem_clear(caches)
    for s in k.layer_sems:
        nc.sync.sem_clear(s)
    nc.all_engine_barrier()


def store_end(k):
    nc, d, ps = k.nc, k.d, k.ps

    @nc_block(nc)
    def _(block):
        @block.tensor
        def _(pe):
            for u in range(8):
                i, g = u // 2, u % 2
                for j in range(4):
                    t = nc.tensor.transpose(ps[:, u, j * P:(j + 1) * P], columns(k.xT[:, 4 * g + j], i // 2, i % 2), k.ident[:])
                t.then_inc(k.z_t, 1)
            for h in range(2):
                for g in range(2):
                    u = 2 * h + g
                    pe.wait_ge(k.z_c, u + 1)
                    for j in range(4):
                        t = nc.tensor.transpose(ps[0:HS, u, j * P:(j + 1) * P], k.xT[:, 4 * g + j, h, HP:HN], k.ident[:])
                    t.then_inc(k.z_t, 1)

        @block.vector
        def _(dve):
            for u in range(12):
                dve.wait_ge(k.z_t, u + 1)
                if u < 8:
                    nc.vector.tensor_copy(k.xin[:, u // 2, 512 * (u % 2):512 * (u % 2) + 512], ps[:, u, :]).then_inc(k.z_c, 1)
                else:
                    w = u - 8
                    nc.vector.tensor_copy(k.xins[0:HS, w // 2, 512 * (w % 2):512 * (w % 2) + 512], ps[0:HS, w, :]).then_inc(k.z_c, 1)

        @block.sync
        def _(sp):
            for i in range(4):
                sp.wait_ge(k.z_c, 2 * i + 2)
                sp.dma_start(d["y_prompt"][0, i * P:(i + 1) * P, :], k.xin[:, i, :]).then_inc(k.z_out, 16)
            for h in range(2):
                sp.wait_ge(k.z_c, 10 + 2 * h)
                sp.dma_start(d["y_sample"][4 * h:4 * h + 4].rearrange("b t d -> (b t) d"), k.xins[0:HS, h, :]).then_inc(k.z_out, 16)
            sp.wait_ge(k.z_out, 16 * 6)


class Tiles:
    pass


def build(nc, dram):
    k = Tiles()
    k.nc, k.d = nc, dram
    d = dram
    with ExitStack() as ctx:
        ctx.enter_context(nc.allow_non_contiguous_dma(reason="small parameters, features onto partitions"))

        def sb(name, shape, dt=F32):
            return ctx.enter_context(nc.sbuf_tensor(name, shape, dt))

        k.ps = ctx.enter_context(nc.psum_tensor("ps", [P, 8, 512], F32))
        k.xT = sb("xT", [P, KD, 2, HN])
        stream = sb("stream", [P, max(SLOTS * SLOT, CACHES * GROUPS * 5 * P)])
        k.ring = stream[:, 0:SLOTS * SLOT].rearrange("p (s n) -> p s n", s=SLOTS)
        k.ident, k.ones, k.rot = sb("ident", [P, P]), sb("ones", [P, P]), sb("rot", [P, P])
        k.rotrep, k.sel = sb("rotrep", [32, P]), sb("sel", [P, 4 * P])
        k.cos, k.sin, k.pcnt = sb("cos", [P, N]), sb("sin", [P, N]), sb("pcnt", [P, 2, 2, HN])
        k.cmask, k.nmask = sb("cmask", [P, P]), sb("nmask", [HS, DB, 32])
        k.row, k.pages, k.idx = sb("row", [P, 1 + 4 + 8]), sb("pages", [P, DB * NPAGE], I32), sb("idx", [P, DB * LOADS], I32)
        k.idxf, k.idxt, k.pick = sb("idxf", [P, DB * LOADS]), sb("idxt", [P, DB * LOADS]), k.row[:, 5:13]
        k.rank = k.row[:, 1:5]
        k.eps, k.prm, k.cw, k.sw = sb("eps", [P, 2]), sb("prm", [P, 44]), sb("cw", [P, 2, CONVK]), sb("sw", [P, 2, SCK])
        k.wuqn, k.wuqr = sb("wuqn", [P, 2, 512]), sb("wuqr", [P, 2, 256])
        k.wuk, k.wuv, k.poolw = sb("wuk", [P, 512]), sb("wuv", [P, NH, P]), sb("poolw", [P, 2, P])
        k.router, k.rbias = sb("router", [P, KD, NG + NE]), sb("rbias", [P, NG + NE])
        k.tail, k.stail = sb("tail", [CONVH, 3, 256]), sb("stail", [HS, 3, 2, 256])
        k.stat = sb("stat", [P, 2])
        ARENA = 22528
        arena = sb("arena", [P, ARENA])
        at = 0

        def take(*shape):
            nonlocal at
            size = 1
            for x in shape:
                size *= x
            assert at + size <= ARENA, (at, shape)
            t = arena[:, at:at + size]
            at += size
            if len(shape) == 1:
                return t
            names = "abcd"[:len(shape)]
            return t.rearrange(f"p ({' '.join(names)}) -> p {' '.join(names)}", **dict(zip(names, shape)))

        k.xin, k.xins = take(4, D), take(2, D)
        at = 0
        k.pooled, k.y, k.dd = take(2, 2, HN), take(2, 2, HN), take(2, 2, HN)
        k.ckvT, k.ckvn, k.ckvs, k.krn, k.krs = take(2, HN), take(4, P), take(2, P), take(4, 32), take(2, 32)
        k.aa, k.bb, k.yc = k.pooled, k.y, k.y
        shared = at
        k.qnope, k.wukT, k.t1, k.t2 = take(4, 2, HN), take(NH, P), take(2, HN), take(2, HN)
        at = shared
        k.lat = take(NH, 2, HN)
        queries = at
        k.sqq, k.sqk, k.sqc = take(2, 2, HN), take(2, HN), take(2, 2, HN)
        k.rq, k.rk, k.rc = take(2, HN), take(2, HN), take(2, HN)
        at = queries
        k.qlat = take(NH, 2, HN)
        k.krpad, k.qr, k.qdr = take(4, 2, HN), take(2, 2, HN), take(DB, 4, 32)
        work = at
        k.qa, k.kva, k.kr = take(2, 2, HN), take(1, 2, HN), take(1, 2, HN)
        at = shared
        k.up_p, k.up_s = take(2, POOLH + SEQ), take(2, DB, POOLH + DS)
        k.wp, k.ws = [take(POOLH + SEQ) for _ in range(2)], [take(DB, POOLH + DS) for _ in range(2)]
        k.glu_p, k.glu_s = take(2, CONVH + SEQ), take(2, DB, CONVH + DS)
        k.v_p, k.v_s = take(2, SCH + SEQ), take(2, DB, SCH + DS)
        k.ga, k.gb, k.cg, k.hh, k.cv = (take(2, 2, HN) for _ in range(5))
        k.kcat = take(3, 2, 2, HS)
        assert at <= work
        at = work + 4 * 2 * HN
        k.hpool, k.hconv, k.hsc = take(256), take(2, 256), take(256)
        at = work
        k.prob, k.probT = take(3, 512), take(2, 512)
        k.mx, k.nm, k.sm, k.rs = (take(32) for _ in range(4))
        at = work
        k.kT, k.krT, k.pd, k.pn = take(2, 512), take(2, 512), take(2, 1024), take(2, 32)
        k.sn, k.mab, k.m1, k.dg, k.mb, k.ss, k.ri = take(DB, 32), take(2, 32), take(32), take(32), take(32), take(32), take(32)
        k.ckv = stream[:, 0:CACHES * GROUPS * 512].rearrange("p (b g n) -> p b g n", b=CACHES, g=GROUPS)
        k.ckr = stream[:, CACHES * GROUPS * 512:].rearrange("p (b g n) -> p b g n", b=CACHES, g=GROUPS)
        at = queries
        k.cc, k.merged, k.sg = take(4, 2, HN), take(KD, 2, HN), take(2, 2, HN)
        at = 0
        k.sq, k.sd = take(2, 2, HN), take(2, HN)
        at = 0
        k.hid = take(2 * NE, 2, HN)
        k.sgf, k.combT = take(3, HN), take(N)
        k.lg, k.comb = sb("lg", [P, 5, 20]), sb("comb", [P, 5, NE])
        k.g1, k.ge, k.es, k.tt, k.o1, k.o2 = (sb(name, [P, 5, 4]) for name in ("g1", "ge", "es", "tt", "o1", "o2"))
        k.gm, k.r1, k.gw, k.b1, k.b2, k.e2 = (sb(name, [P, 5]) for name in ("gm", "r1", "gw", "b1", "b2", "e2"))
        k.n_pool = d["cache_ckv"].shape[1]
        k.ckv_table = d["cache_ckv"].rearrange("l n (r j) c -> (l n r) (j c)", j=8)
        k.kr_table = d["cache_krope"].rearrange("l n (r j) c -> (l n r) (j c)", j=8)

        def sem(name):
            return ctx.enter_context(nc.semaphore(name))

        k.layer_sems = []

        def layer(name):
            k.layer_sems.append(sem(name))
            return k.layer_sems[-1]

        k.s_const, k.s_set, k.s_xt, k.s_xc, k.s_idx, k.z_t, k.z_c, k.z_out = sem("s_const"), sem("s_set"), sem("s_xt"), sem("s_xc"), sem("s_idx"), sem("z_t"), sem("z_c"), sem("z_out")
        k.s_x = [sem(f"s_x{i}") for i in range(5)]
        k.w_free = layer("w_free")
        k.s_hist, k.s_prm, k.s_prm2, k.s_out, k.s_kept = layer("s_hist"), layer("s_prm"), layer("s_prm2"), layer("s_out"), layer("s_kept")
        k.a_mm, k.a_evac, k.a_zero, k.a_done, k.a_chain = layer("a_mm"), layer("a_evac"), layer("a_zero"), layer("a_done"), layer("a_chain")
        k.b_mm, k.b_A, k.b_D, k.b_zero, k.b_sq = layer("b_mm"), layer("b_A"), layer("b_D"), layer("b_zero"), layer("b_sq")
        k.b_yc, k.b_z, k.b_qn, k.b_ckv, k.b_kr = layer("b_yc"), layer("b_z"), layer("b_qn"), layer("b_ckv"), layer("b_kr")
        k.b_qr, k.b_chA, k.b_chD = layer("b_qr"), layer("b_chA"), layer("b_chD")
        k.c_s, k.c_t, k.c_v, k.c_m, k.c_exp = layer("c_s"), layer("c_t"), layer("c_v"), layer("c_m"), layer("c_exp")
        k.c_pn, k.c_pt, k.c_lat, k.c_chain = layer("c_pn"), layer("c_pt"), layer("c_lat"), layer("c_chain")
        k.d_sn, k.d_krt, k.d_krc, k.d_kt, k.d_kc = layer("d_sn"), layer("d_krt"), layer("d_krc"), layer("d_kt"), layer("d_kc")
        k.d_s, k.d_m1, k.d_mt, k.d_dg, k.d_mb = layer("d_s"), layer("d_m1"), layer("d_mt"), layer("d_dg"), layer("d_mb")
        k.d_sub, k.d_pn, k.d_exp, k.d_ss, k.d_sd = layer("d_sub"), layer("d_pn"), layer("d_exp"), layer("d_ss"), layer("d_sd")
        k.d_pv, k.d_lat, k.d_chain = layer("d_pv"), layer("d_lat"), layer("d_chain")
        k.e_cm, k.e_c, k.e_g, k.e_sg, k.e_p = layer("e_cm"), layer("e_c"), layer("e_g"), layer("e_sg"), layer("e_p")
        k.e_mg, k.e_t, k.e_o, k.e_z = layer("e_mg"), layer("e_t"), layer("e_o"), layer("e_z")
        k.f_lg, k.f_u, k.f_h, k.f_w, k.f_cb = layer("f_lg"), layer("f_u"), layer("f_h"), layer("f_w"), layer("f_cb")
        k.f_ct, k.f_cc, k.f_d, k.f_z, k.f_sg = layer("f_ct"), layer("f_cc"), layer("f_d"), layer("f_z"), layer("f_sg")
        k.f_t, k.f_r, k.f_ra, k.f_chain = layer("f_t"), layer("f_r"), layer("f_ra"), layer("f_chain")
        k.w_in = [sem(f"w_in{i}") for i in range(SLOTS)]
        k.c_in = [sem(f"c_in{i}") for i in range(CACHES * LOADS)]
        k.c_inr = [sem(f"c_inr{i}") for i in range(CACHES * LOADS)]
        assert [s.num for s in k.c_in + k.c_inr] == list(range(k.c_in[0].num, k.c_in[0].num + 2 * CACHES * LOADS))
        k.layer_sems += k.w_in
        norms = []
        for n in range(2):
            s = Tiles()
            s.mean, s.c, s.sq, s.var = layer(f"n{n}_mean"), layer(f"n{n}_c"), layer(f"n{n}_sq"), layer(f"n{n}_var")
            s.sd, s.r, s.n, s.x = layer(f"n{n}_sd"), layer(f"n{n}_r"), layer(f"n{n}_n"), layer(f"n{n}_x")
            norms.append(s)

        load_start(k)
        with nc.Fori(0, DEPTH) as l:
            project(k, l)
            attend_inputs(k, l)
            attend_prompt(k, l)
            attend_sample(k, l)
            merge(k, l)
            layer_norm(k, norms[0], 0, 8)
            experts(k, l)
            layer_norm(k, norms[1], 16, 24)
            end_layer(k)
        store_end(k)


INS = ['x_prompt', 'x_sample', 'cache_ckv', 'cache_krope', 'state_pool', 'state_conv', 'state_sconv', 'page_table',
       'ln1_g', 'ln1_b', 'ln2_g', 'ln2_b', 'w_in', 'pool_w', 'pool_scale', 'conv_w', 'conv_b', 'conv_ln_g', 'conv_ln_b',
       'q_norm_g', 'kv_norm_g', 'w_uq', 'w_uk', 'w_uv', 'sconv_w', 'p_pool', 'p_conv', 'p_attn', 'p_sconv', 'w_o',
       'router_g', 'router_g_b', 'router_e', 'router_e_b', 'exp_w_gate', 'exp_w_up', 'exp_w_down']
OUTS = [('y_prompt', (1, SEQ, D)), ('y_sample', (DB, DS, D)),
        ('new_ckv_prompt', (DEPTH, 1, SEQ, KVL)), ('new_krope_prompt', (DEPTH, 1, SEQ, ROPE)),
        ('new_pool_prompt', (DEPTH, 1, POOLH, POOLW)), ('new_conv_prompt', (DEPTH, 1, CONVH, CONVW)),
        ('new_sconv_prompt', (DEPTH, 1, SCH, SCW)),
        ('new_ckv_sample', (DEPTH, DB, DS, KVL)), ('new_krope_sample', (DEPTH, DB, DS, ROPE)),
        ('new_pool_sample', (DEPTH, DB, POOLH, POOLW)), ('new_conv_sample', (DEPTH, DB, CONVH, CONVW)),
        ('new_sconv_sample', (DEPTH, DB, SCH, SCW))]


def constants():
    import numpy as np

    f = np.float32
    past = PAGE * NPAGE
    half = np.concatenate([np.arange(HP), past + np.arange(HS) % DS])
    pos = np.concatenate([half, np.concatenate([HP + np.arange(HP), past + np.arange(HS) % DS])])
    inv = f(10000.0) ** (-np.arange(ROPE // 2, dtype=f) / f(ROPE // 2))
    ang = (pos.astype(f)[None, :] * inv[np.arange(P) % (ROPE // 2)][:, None]).astype(f)
    rot, rotrep, sel = np.zeros((P, P), f), np.zeros((32, P), f), np.zeros((P, 4, P), f)
    for m in range(P):
        up = m % 32 < 16
        rot[m + 16 if up else m - 16, m] = -1.0 if up else 1.0
        rotrep[m % 32 + 16 if up else m % 32 - 16, m] = -1.0 if up else 1.0
        for j in range(4):
            sel[32 * j + m % 32, j, m] = 1.0
    pcnt = np.zeros((P, 2, N), f)
    for c in range(2):
        for g in range(2):
            win = 2 << (2 * c + g)
            pcnt[64 * g:64 * g + 64, c, :] = (f(1.0) / np.minimum(win, pos + 1).astype(f))[None, :]
    i = np.arange(P)
    cmask = np.where(i[:, None] >= i[None, :], f(0), f(NEG)).astype(f)
    nmask = np.full((HS, DB, NH, DS), NEG, f)
    for b in range(DB):
        for t in range(DS):
            for q in range(t, DS):
                nmask[DS * (b % 4) + t, b, :, q] = 0.0
    row = np.zeros((P, 13), f)
    row[:, 0] = i % 16
    row[i, 5 + i // 16] = 1
    row[:, 1:5] = [4, 3, 2, 1]
    return {"c_ident": np.eye(P, dtype=f), "c_rot": rot, "c_rotrep": rotrep, "c_sel": sel.reshape(P, 4 * P),
            "c_cos": np.cos(ang), "c_sin": np.sin(ang), "c_pcnt": pcnt.reshape(P, 2, 2, HN), "c_cmask": cmask,
            "c_nmask": nmask.reshape(HS, DB, 32), "c_row": row}


def kernel(**inputs):
    import numpy as np
    import concourse.bacc as bacc
    from concourse.bass_utils import run_bass_kernel_spmd

    nc = bacc.Bacc("TRN2", target_bir_lowering=False, num_devices=1)
    arrays, dram = {}, {}
    for name, a in list((n, inputs[n]) for n in INS) + list(constants().items()):
        a = np.ascontiguousarray(a)
        arrays[f"in_{name}"] = a
        dram[name] = nc.dram_tensor(f"in_{name}", a.shape, mybir.dt.from_np(a.dtype), kind="ExternalInput").ap()
    for name, shape in OUTS:
        dram[name] = nc.dram_tensor(f"out_{name}", shape, F32, kind="ExternalOutput").ap()
    build(nc, dram)
    r = run_bass_kernel_spmd(nc, [arrays], core_ids=[0])
    return tuple(r.results[0][f"out_{name}"] for name, _ in OUTS)
```
